# Optimizing a Trainium2 kernel written in Bass

```python
import jax, jax.numpy as jnp
from jax import lax
import numpy as np
import math

D_MODEL = 2048
BATCH = 1
SEQ = 256
DEPTH = 1

N_BRANCH = 4
BRANCH_WIDTH = D_MODEL // 4
LRU_WIDTH = BRANCH_WIDTH
LRU_BLOCKS = 8
LRU_BLOCK_DIM = LRU_WIDTH // LRU_BLOCKS
LRU_CONV = 4
LRU_C = 8.0
POOL_WIDTH = BRANCH_WIDTH
POOL_WINDOWS = (2, 4, 8, 16)
POOL_GROUPS = 4
POOL_GROUP_DIM = POOL_WIDTH // POOL_GROUPS
SCONV_WIDTH = BRANCH_WIDTH
SCONV_K = 3
ATTN_HEADS = 8
HEAD_DIM = BRANCH_WIDTH // ATTN_HEADS
ATTN_WIDTH = ATTN_HEADS * HEAD_DIM
Q_BLOCK = 128
D_FF = 4 * D_MODEL
EPS = 1e-6
IN_SIZES = (LRU_WIDTH, POOL_WIDTH, 3 * SCONV_WIDTH, 3 * ATTN_WIDTH, ATTN_HEADS, N_BRANCH * D_MODEL)
N_IN = sum(IN_SIZES)


def _split_points():
    return [int(v) for v in np.cumsum(IN_SIZES)[:-1]]

def rms_norm(x, g):
    xf = x.astype(jnp.float32)
    y = xf * lax.rsqrt(jnp.mean(xf * xf, axis=-1, keepdims=True) + EPS)
    return (y * g.astype(jnp.float32)).astype(x.dtype)

def causal_depthwise_conv(x, w):
    k_width = w.shape[0]
    s = x.shape[1]
    xp = jnp.pad(x, ((0, 0), (k_width - 1, 0), (0, 0)))
    return sum(w[k] * xp[:, k:k + s] for k in range(k_width))

def rglru_branch(xa, conv_w, conv_b, wr, br, wi, bi, lam):
    b, s, _ = xa.shape
    u = causal_depthwise_conv(xa, conv_w) + conv_b
    ub = u.reshape(b, s, LRU_BLOCKS, LRU_BLOCK_DIM)
    r = jax.nn.sigmoid(jnp.einsum('bshi,hij->bshj', ub, wr).reshape(b, s, LRU_WIDTH) + br)
    gi = jax.nn.sigmoid(jnp.einsum('bshi,hij->bshj', ub, wi).reshape(b, s, LRU_WIDTH) + bi)
    log_a = (-LRU_C * r.astype(jnp.float32)) * jax.nn.softplus(-lam.astype(jnp.float32))
    a = jnp.exp(log_a)
    inp = jnp.sqrt(-jnp.expm1(2.0 * log_a)) * (gi * u).astype(jnp.float32)

    def combine(c1, c2):
        a1, b1 = c1
        a2, b2 = c2
        return a1 * a2, a2 * b1 + b2

    _, h = lax.associative_scan(combine, (a, inp), axis=1)
    return h.astype(xa.dtype)

def pool_branch(xp, w_grp, scale):
    b, s, _ = xp.shape
    xf = xp.astype(jnp.float32)
    csum = jnp.pad(jnp.cumsum(xf, axis=1), ((0, 0), (1, 0), (0, 0)))
    t = jnp.arange(s)
    outs = []
    for gidx, win in enumerate(POOL_WINDOWS):
        sl = slice(gidx * POOL_GROUP_DIM, (gidx + 1) * POOL_GROUP_DIM)
        start = jnp.maximum(t + 1 - win, 0)
        win_sum = csum[:, 1:, sl] - csum[:, start, sl]
        count = jnp.minimum(t + 1, win).astype(jnp.float32)[None, :, None]
        outs.append(win_sum / count - xf[:, :, sl])
    pooled = jnp.stack(outs, axis=2)
    mixed = jnp.einsum('bsgi,gij->bsgj', pooled, w_grp.astype(jnp.float32)).reshape(b, s, POOL_WIDTH)
    return (mixed * scale.astype(jnp.float32)).astype(xp.dtype)

def shortconv_branch(xsc, w):
    gate_b, gate_c, xc = jnp.split(xsc, 3, axis=-1)
    return gate_b * causal_depthwise_conv(gate_c * xc, w)

def forgetting_attention(qkv, f_logit, f_bias, q_g, k_g):
    b, s, _ = qkv.shape
    q, k, v = jnp.split(qkv, 3, axis=-1)
    q = rms_norm(q.reshape(b, s, ATTN_HEADS, HEAD_DIM), q_g)
    k = rms_norm(k.reshape(b, s, ATTN_HEADS, HEAD_DIM), k_g)
    v = v.reshape(b, s, ATTN_HEADS, HEAD_DIM)
    log_f = jax.nn.log_sigmoid((f_logit + f_bias).astype(jnp.float32))
    cum = jnp.cumsum(log_f, axis=1).transpose(0, 2, 1)
    n_blk = s // Q_BLOCK
    qb = q.reshape(b, n_blk, Q_BLOCK, ATTN_HEADS, HEAD_DIM).transpose(1, 0, 2, 3, 4)
    cqb = cum.reshape(b, ATTN_HEADS, n_blk, Q_BLOCK).transpose(2, 0, 1, 3)
    key_pos = jnp.arange(s)
    scale = HEAD_DIM ** -0.5

    def one_block(args):
        qi, cqi, blk = args
        logits = jnp.einsum('bqhd,bkhd->bhqk', qi, k).astype(jnp.float32) * scale
        logits = logits + (cqi[..., :, None] - cum[..., None, :])
        q_pos = blk * Q_BLOCK + jnp.arange(Q_BLOCK)
        logits = jnp.where(key_pos[None, :] <= q_pos[:, None], logits, -jnp.inf)
        p = jax.nn.softmax(logits, axis=-1)
        return jnp.einsum('bhqk,bkhd->bqhd', p.astype(v.dtype), v)

    out = lax.map(one_block, (qb, cqb, jnp.arange(n_blk)))
    return out.transpose(1, 0, 2, 3, 4).reshape(b, s, ATTN_WIDTH)

def first_inputs(seed: int = 0) -> dict:
    key = jax.random.key(seed)
    ks = jax.random.split(key, 24)
    L, D, W = DEPTH, D_MODEL, BRANCH_WIDTH
    nrm = lambda k, shape, fan: jax.random.normal(k, shape, jnp.float32) * (fan ** -0.5)
    u = jax.random.uniform(ks[9], (L, LRU_WIDTH), jnp.float32, 0.9, 0.999)
    a0 = u ** (1.0 / LRU_C)
    return {
        "x": jax.random.normal(ks[0], (BATCH, SEQ, D), jnp.float32),
        "norm_mix_g": 1.0 + 0.1 * jax.random.normal(ks[1], (L, D), jnp.float32),
        "w_in": nrm(ks[2], (L, D, N_IN), D),
        "lru_conv_w": nrm(ks[3], (L, LRU_CONV, LRU_WIDTH), LRU_CONV),
        "lru_conv_b": 0.02 * jax.random.normal(ks[4], (L, LRU_WIDTH), jnp.float32),
        "lru_wr": nrm(ks[5], (L, LRU_BLOCKS, LRU_BLOCK_DIM, LRU_BLOCK_DIM), LRU_BLOCK_DIM),
        "lru_br": 0.02 * jax.random.normal(ks[6], (L, LRU_WIDTH), jnp.float32),
        "lru_wi": nrm(ks[7], (L, LRU_BLOCKS, LRU_BLOCK_DIM, LRU_BLOCK_DIM), LRU_BLOCK_DIM),
        "lru_bi": 0.02 * jax.random.normal(ks[8], (L, LRU_WIDTH), jnp.float32),
        "lru_lambda": jnp.log(a0) - jnp.log1p(-a0),
        "pool_w": nrm(ks[10], (L, POOL_GROUPS, POOL_GROUP_DIM, POOL_GROUP_DIM), POOL_GROUP_DIM),
        "pool_scale": 1.0 + 0.1 * jax.random.normal(ks[11], (L, POOL_WIDTH), jnp.float32),
        "sconv_w": nrm(ks[12], (L, SCONV_K, SCONV_WIDTH), SCONV_K),
        "q_norm_g": 1.0 + 0.1 * jax.random.normal(ks[13], (L, HEAD_DIM), jnp.float32),
        "k_norm_g": 1.0 + 0.1 * jax.random.normal(ks[14], (L, HEAD_DIM), jnp.float32),
        "forget_b": jax.random.uniform(ks[15], (L, ATTN_HEADS), jnp.float32, 1.0, 5.0),
        "w_branch": nrm(ks[16], (L, N_BRANCH, W, D), W),
        "w_out": nrm(ks[17], (L, D, D), D),
        "norm_mlp_g": 1.0 + 0.1 * jax.random.normal(ks[18], (L, D), jnp.float32),
        "w_mlp_up": nrm(ks[19], (L, D, D_FF), D),
        "w_mlp_down": nrm(ks[20], (L, D_FF, D), D_FF),
    }

def first_block(x, norm_mix_g, w_in, lru_conv_w, lru_conv_b, lru_wr, lru_br, lru_wi, lru_bi,
              lru_lambda, pool_w, pool_scale, sconv_w, q_norm_g, k_norm_g, forget_b,
              w_branch, w_out, norm_mlp_g, w_mlp_up, w_mlp_down):
    b, s, d = x.shape
    split_pts = _split_points()
    for l in range(DEPTH):
        xn = rms_norm(x, norm_mix_g[l])
        proj = xn @ w_in[l]
        xa, xpool, xsc, qkv, f_logit, gate_logits = jnp.split(proj, split_pts, axis=-1)
        y_a = rglru_branch(xa, lru_conv_w[l], lru_conv_b[l], lru_wr[l], lru_br[l],
                           lru_wi[l], lru_bi[l], lru_lambda[l])
        y_b = pool_branch(xpool, pool_w[l], pool_scale[l])
        y_c = shortconv_branch(xsc, sconv_w[l])
        y_d = forgetting_attention(qkv, f_logit, forget_b[l], q_norm_g[l], k_norm_g[l])
        ys = jnp.stack([y_a, y_b, y_c, y_d], axis=2)
        branches = jnp.einsum('bskw,kwd->bskd', ys, w_branch[l])
        gates = jax.nn.sigmoid(gate_logits.reshape(b, s, N_BRANCH, d))
        merged = jnp.sum(gates * branches, axis=2)
        x = x + merged @ w_out[l]
        h = rms_norm(x, norm_mlp_g[l]) @ w_mlp_up[l]
        x = x + jnp.square(jax.nn.relu(h)) @ w_mlp_down[l]
    return x


MIX_WIDTH = D_MODEL // 2
N_BRANCHES = 3
CHUNK = 128
GM_WIDTH = MIX_WIDTH
GM_GROUP_CH = 128
GM_GROUPS = GM_WIDTH // GM_GROUP_CH
S5_WIDTH = MIX_WIDTH
S5_GROUP_CH = 16
S5_GROUPS = S5_WIDTH // S5_GROUP_CH
S5_STATE = 64
DT_MIN = 1e-3
DT_MAX = 1e-1
SB_WIDTH = MIX_WIDTH
SB_HEAD_DIM = 128
SB_HEADS = SB_WIDTH // SB_HEAD_DIM
SB_BLOCK = 128
PROJ_COLS = 2 * GM_WIDTH + S5_WIDTH + 3 * SB_WIDTH + N_BRANCHES * D_MODEL
D_FF_2 = 4 * D_MODEL


def rmsnorm(x, g):
    xf = x.astype(jnp.float32)
    y = xf * lax.rsqrt(jnp.mean(xf * xf, axis=-1, keepdims=True) + EPS)
    return (y * g.astype(jnp.float32)).astype(x.dtype)

def gmlp_mixer(uv, norm_g, w_s, b_s):
    bsz, seq, _ = uv.shape
    z = jax.nn.gelu(uv)
    u, v = jnp.split(z, 2, axis=-1)
    v = rmsnorm(v, norm_g)
    v = v.reshape(bsz, seq // CHUNK, CHUNK, GM_GROUPS, GM_GROUP_CH)
    w = jnp.tril(w_s)
    mixed = jnp.einsum('gts,bcsgh->bctgh', w, v) + jnp.transpose(b_s)[None, None, :, :, None]
    return u * mixed.reshape(bsz, seq, GM_WIDTH)

def s5_mixer(xin, lam_re, lam_im, log_dt, b_re, b_im, c_re, c_im, d, w_glu, b_glu):
    f32 = jnp.float32
    bsz, seq, _ = xin.shape
    u = xin.astype(f32).reshape(bsz, seq, S5_GROUPS, S5_GROUP_CH)
    lam_re = lam_re.astype(f32)
    lam_im = lam_im.astype(f32)
    b_re = b_re.astype(f32)
    b_im = b_im.astype(f32)
    dt = jnp.exp(log_dt.astype(f32))[:, None]
    mag = jnp.exp(lam_re * dt)
    ab_re = mag * jnp.cos(lam_im * dt)
    ab_im = mag * jnp.sin(lam_im * dt)
    den = lam_re * lam_re + lam_im * lam_im
    n_re = ab_re - 1.0
    n_im = ab_im
    k_re = (n_re * lam_re + n_im * lam_im) / den
    k_im = (n_im * lam_re - n_re * lam_im) / den
    bb_re = k_re[..., None] * b_re - k_im[..., None] * b_im
    bb_im = k_re[..., None] * b_im + k_im[..., None] * b_re
    bu_re = jnp.einsum('blgh,gph->blgp', u, bb_re)
    bu_im = jnp.einsum('blgh,gph->blgp', u, bb_im)
    a_re = jnp.broadcast_to(ab_re, bu_re.shape)
    a_im = jnp.broadcast_to(ab_im, bu_im.shape)

    def combine(e_i, e_j):
        ar_i, ai_i, br_i, bi_i = e_i
        ar_j, ai_j, br_j, bi_j = e_j
        return (ar_j * ar_i - ai_j * ai_i,
                ar_j * ai_i + ai_j * ar_i,
                ar_j * br_i - ai_j * bi_i + br_j,
                ar_j * bi_i + ai_j * br_i + bi_j)

    _, _, s_re, s_im = lax.associative_scan(combine, (a_re, a_im, bu_re, bu_im), axis=1)
    y = (jnp.einsum('blgp,ghp->blgh', s_re, c_re.astype(f32))
         - jnp.einsum('blgp,ghp->blgh', s_im, c_im.astype(f32)))
    y = y.reshape(bsz, seq, S5_WIDTH) + d.astype(f32) * xin.astype(f32)
    g = jax.nn.gelu(y)
    out = g * jax.nn.sigmoid(g @ w_glu.astype(f32) + b_glu.astype(f32))
    return out.astype(xin.dtype)

def stick_breaking_attention(q, k, v):
    f32 = jnp.float32
    seq = q.shape[2]
    scale = SB_HEAD_DIM ** -0.5
    outs = []
    for blk in range(seq // SB_BLOCK):
        t0 = blk * SB_BLOCK
        t1 = t0 + SB_BLOCK
        qb = q[:, :, t0:t1].astype(f32)
        kb = k[:, :, :t1].astype(f32)
        vb = v[:, :, :t1].astype(f32)
        z = jnp.einsum('bhtd,bhsd->bhts', qb, kb) * scale
        mask = jnp.arange(t1)[None, :] < jnp.arange(t0, t1)[:, None]
        log_1m = jnp.where(mask, jax.nn.log_sigmoid(-z), 0.0)
        after = lax.cumsum(log_1m, axis=3, reverse=True) - log_1m
        w = jnp.where(mask, jnp.exp(jax.nn.log_sigmoid(z) + after), 0.0)
        outs.append(jnp.einsum('bhts,bhsd->bhtd', w, vb))
    return jnp.concatenate(outs, axis=2).astype(q.dtype)

def second_inputs(seed: int = 0) -> dict:
    key = jax.random.key(seed)
    ks = jax.random.split(key, 32)

    def nrm(k, shape, scale):
        return jax.random.normal(k, shape, jnp.float32) * scale

    x = nrm(ks[0], (BATCH, SEQ, D_MODEL), 1.0)
    norm1_g = 1.0 + nrm(ks[1], (DEPTH, D_MODEL), 0.05)
    w_in = nrm(ks[2], (DEPTH, D_MODEL, PROJ_COLS), D_MODEL ** -0.5)
    b_gate = nrm(ks[3], (DEPTH, N_BRANCHES, D_MODEL), 0.1)
    gm_norm_g = 1.0 + nrm(ks[4], (DEPTH, GM_WIDTH), 0.05)
    gm_w_s = nrm(ks[5], (DEPTH, GM_GROUPS, CHUNK, CHUNK), CHUNK ** -0.5)
    gm_b_s = 1.0 + nrm(ks[6], (DEPTH, GM_GROUPS, CHUNK), 0.1)
    s5_lambda_re = -0.5 + nrm(ks[7], (DEPTH, S5_GROUPS, S5_STATE), 0.01)
    s5_lambda_im = (math.pi * jnp.arange(S5_STATE, dtype=jnp.float32))[None, None, :] \
        + nrm(ks[8], (DEPTH, S5_GROUPS, S5_STATE), 0.01)
    s5_log_dt = jax.random.uniform(ks[9], (DEPTH, S5_GROUPS), jnp.float32,
                                   math.log(DT_MIN), math.log(DT_MAX))
    s5_b_re = nrm(ks[10], (DEPTH, S5_GROUPS, S5_STATE, S5_GROUP_CH), (2 * S5_GROUP_CH) ** -0.5)
    s5_b_im = nrm(ks[11], (DEPTH, S5_GROUPS, S5_STATE, S5_GROUP_CH), (2 * S5_GROUP_CH) ** -0.5)
    s5_c_re = nrm(ks[12], (DEPTH, S5_GROUPS, S5_GROUP_CH, S5_STATE), (2 * S5_STATE) ** -0.5)
    s5_c_im = nrm(ks[13], (DEPTH, S5_GROUPS, S5_GROUP_CH, S5_STATE), (2 * S5_STATE) ** -0.5)
    s5_d = nrm(ks[14], (DEPTH, S5_WIDTH), 1.0)
    s5_w_glu = nrm(ks[15], (DEPTH, S5_WIDTH, S5_WIDTH), S5_WIDTH ** -0.5)
    s5_b_glu = nrm(ks[16], (DEPTH, S5_WIDTH), 0.02)
    w_branch = nrm(ks[17], (DEPTH, N_BRANCHES, MIX_WIDTH, D_MODEL), MIX_WIDTH ** -0.5)
    w_out = nrm(ks[18], (DEPTH, D_MODEL, D_MODEL), D_MODEL ** -0.5)
    norm2_g = 1.0 + nrm(ks[19], (DEPTH, D_MODEL), 0.05)
    w_mlp_in = nrm(ks[20], (DEPTH, D_MODEL, D_FF_2), D_MODEL ** -0.5)
    w_mlp_out = nrm(ks[21], (DEPTH, D_FF_2, D_MODEL), D_FF_2 ** -0.5)
    final_g = 1.0 + nrm(ks[22], (D_MODEL,), 0.05)
    return {"x": x, "norm1_g": norm1_g, "w_in": w_in, "b_gate": b_gate,
            "gm_norm_g": gm_norm_g, "gm_w_s": gm_w_s, "gm_b_s": gm_b_s,
            "s5_lambda_re": s5_lambda_re, "s5_lambda_im": s5_lambda_im, "s5_log_dt": s5_log_dt,
            "s5_b_re": s5_b_re, "s5_b_im": s5_b_im, "s5_c_re": s5_c_re, "s5_c_im": s5_c_im,
            "s5_d": s5_d, "s5_w_glu": s5_w_glu, "s5_b_glu": s5_b_glu,
            "w_branch": w_branch, "w_out": w_out, "norm2_g": norm2_g,
            "w_mlp_in": w_mlp_in, "w_mlp_out": w_mlp_out, "final_g": final_g}

def second_block(x, norm1_g, w_in, b_gate, gm_norm_g, gm_w_s, gm_b_s,
              s5_lambda_re, s5_lambda_im, s5_log_dt, s5_b_re, s5_b_im, s5_c_re, s5_c_im,
              s5_d, s5_w_glu, s5_b_glu, w_branch, w_out, norm2_g,
              w_mlp_in, w_mlp_out, final_g):
    bsz, seq, _ = x.shape
    o_a = 2 * GM_WIDTH
    o_b = o_a + S5_WIDTH
    o_c = o_b + 3 * SB_WIDTH
    for l in range(DEPTH):
        h = rmsnorm(x, norm1_g[l])
        proj = h @ w_in[l]
        uv = proj[..., :o_a]
        s5_in = proj[..., o_a:o_b]
        qkv = proj[..., o_b:o_c].reshape(bsz, seq, 3, SB_HEADS, SB_HEAD_DIM)
        qkv = jnp.transpose(qkv, (2, 0, 3, 1, 4))
        gates = jax.nn.sigmoid(proj[..., o_c:].reshape(bsz, seq, N_BRANCHES, D_MODEL) + b_gate[l])

        y_a = gmlp_mixer(uv, gm_norm_g[l], gm_w_s[l], gm_b_s[l])
        y_b = s5_mixer(s5_in, s5_lambda_re[l], s5_lambda_im[l], s5_log_dt[l],
                       s5_b_re[l], s5_b_im[l], s5_c_re[l], s5_c_im[l],
                       s5_d[l], s5_w_glu[l], s5_b_glu[l])
        y_c = stick_breaking_attention(qkv[0], qkv[1], qkv[2])
        y_c = jnp.transpose(y_c, (0, 2, 1, 3)).reshape(bsz, seq, SB_WIDTH)

        ys = jnp.stack([y_a, y_b, y_c], axis=2)
        br = jnp.einsum('blnw,nwd->blnd', ys, w_branch[l])
        merged = jnp.sum(gates * br, axis=2)
        x = x + merged @ w_out[l]
        h2 = rmsnorm(x, norm2_g[l])
        x = x + jnp.square(jax.nn.relu(h2 @ w_mlp_in[l])) @ w_mlp_out[l]
    return rmsnorm(x, final_g)


def setup_inputs(seed=0):
    out = dict(first_inputs(seed))
    for name, value in second_inputs(seed + 1).items():
        if name != "x":
            out[name + "_2"] = value
    return out


def reference(
    x, norm_mix_g, w_in, lru_conv_w, lru_conv_b, lru_wr, lru_br, lru_wi, lru_bi, lru_lambda,
    pool_w, pool_scale, sconv_w, q_norm_g, k_norm_g, forget_b, w_branch, w_out, norm_mlp_g,
    w_mlp_up, w_mlp_down, norm1_g_2, w_in_2, b_gate_2, gm_norm_g_2, gm_w_s_2, gm_b_s_2,
    s5_lambda_re_2, s5_lambda_im_2, s5_log_dt_2, s5_b_re_2, s5_b_im_2, s5_c_re_2, s5_c_im_2,
    s5_d_2, s5_w_glu_2, s5_b_glu_2, w_branch_2, w_out_2, norm2_g_2, w_mlp_in_2, w_mlp_out_2,
    final_g_2,
):
    x = first_block(
        x, norm_mix_g, w_in, lru_conv_w, lru_conv_b, lru_wr, lru_br, lru_wi, lru_bi, lru_lambda,
        pool_w, pool_scale, sconv_w, q_norm_g, k_norm_g, forget_b, w_branch, w_out, norm_mlp_g,
        w_mlp_up, w_mlp_down,
    )
    return second_block(
        x, norm1_g_2, w_in_2, b_gate_2, gm_norm_g_2, gm_w_s_2, gm_b_s_2, s5_lambda_re_2,
        s5_lambda_im_2, s5_log_dt_2, s5_b_re_2, s5_b_im_2, s5_c_re_2, s5_c_im_2, s5_d_2,
        s5_w_glu_2, s5_b_glu_2, w_branch_2, w_out_2, norm2_g_2, w_mlp_in_2, w_mlp_out_2,
        final_g_2,
    )


_drawn_inputs = setup_inputs


def setup_inputs(seed=0):
    import zlib

    import numpy as np

    out = dict(_drawn_inputs(seed))
    spreads = {}
    factors = {'lru_br': 32.478,
     'lru_bi': 22.932,
     'q_norm_g': 4.41,
     'k_norm_g': 4.533,
     'norm1_g_2': 2.731,
     'b_gate_2': 4.159,
     'gm_norm_g_2': 8.0,
     'gm_b_s_2': 3.024,
     's5_lambda_re_2': 64.0,
     's5_lambda_im_2': 64.0,
     's5_log_dt_2': 64.0,
     's5_b_re_2': 64.0,
     's5_b_im_2': 64.0,
     's5_c_re_2': 64.0,
     's5_c_im_2': 64.0,
     's5_b_glu_2': 64.0,
     'norm2_g_2': 5.715}
    for name, (base, spread) in spreads.items():
        noise = np.random.default_rng([zlib.crc32(name.encode()), seed]).standard_normal(out[name].shape)
        drawn = base * np.exp(spread * noise) if base else spread * noise
        out[name] = __import__('jax').numpy.asarray(drawn.astype(out[name].dtype))
    for name, factor in factors.items():
        out[name] = (out[name] * factor).astype(out[name].dtype)
    return out
```

```python
import concourse.bass as bass
from concourse import mybir
from contextlib import ExitStack

F32 = mybir.dt.float32
F32R = mybir.dt.float32r
ACT = mybir.ActivationFunctionType
ALU = mybir.AluOpType
AX = mybir.AxisListType.X

P = 128
T = 256
NT = T // P
D = 2048
KD = D // P
CH = 512
UK = 2
NCH = D // CH
FF = 8192
NF = FF // CH
RING = 4
EPS = 1e-6
SL = 1024
NEG = -1.0e30
MODE = "both"


class Steps:

    def __init__(self, gen):
        self.gen = gen
        self.at = next(gen, None)

    def upto(self, p):
        while self.at is not None and self.at <= p:
            self.at = next(self.gen, None)


def build(nc, A, out):
    with ExitStack() as ctx:
        def sb(name, shape, dt=F32):
            return ctx.enter_context(nc.sbuf_tensor(name, shape, dt))

        sems = {}

        def S(name):
            if name not in sems:
                sems[name] = ctx.enter_context(nc.semaphore(name))
            return sems[name]

        raw = sb("raw", [P, RING, UK * CH])
        whi = sb("whi", [P, RING, UK * CH], F32R)
        wlo = sb("wlo", [P, RING, UK * CH], F32R)
        XH = sb("XH", [P, KD, T], F32R)
        XL = sb("XL", [P, KD, T], F32R)
        NY = 24
        with nc.sbuf_tensor("Z", [P, 2 * NY * T], F32) as Z:
            pass
        Y = sb("Y", [P, 2 * NY * T], F32R)
        YH = Y[:, 0:NY * T].rearrange("p (k t) -> p k t", t=T)
        YL = Y[:, NY * T:2 * NY * T].rearrange("p (k t) -> p k t", t=T)
        G = sb("G", [P, 4 * SL])
        NA = 14
        W = sb("W", [P, NA * SL])
        ident = sb("ident", [P, P])
        UP = sb("UP", [P, T])
        NLOW = sb("NLOW", [P, P])
        CM = sb("CM", [P, P])
        SM = sb("SM", [P, P])
        S01 = sb("S01", [P, P])
        NONE = sb("NONE", [P, P])
        small = sb("small", [P, 400])
        qg = sb("qg", [P, 2, 64])
        wf = sb("wf", [P, KD, 8])
        wfh = sb("wfh", [P, KD, 8], F32R)
        wfl = sb("wfl", [P, KD, 8], F32R)

        banks = ctx.enter_context(nc.psum_tensor("banks", [P, 8, CH], F32))
        PA = [[banks[:, 2 * b + t, :] for t in range(NT)] for b in range(2)]
        PU = [banks[:, 4 + t, :] for t in range(NT)]
        PT = [banks[:, 6 + t, :] for t in range(NT)]

        off = [0]

        def vec(n):
            off[0] += n
            return small[:, off[0] - n:off[0]]

        ss, rs = vec(2), vec(2)
        vA, vB = vec(P), vec(96)
        conv_w, conv_b, br, bi, lam = vA[:, 0:16], vA[:, 16:20], vA[:, 20:24], vA[:, 24:28], vA[:, 28:32]
        pscale, sconv_w = vA[:, 32:36], vA[:, 36:48]
        s5_d, b_glu, gm_b, even = vA[:, 48:56], vA[:, 56:64], vA[:, 64:72], vA[:, 96:97]
        lam_re, lam_im, log_dt = vB[:, 0:32], vB[:, 32:64], vB[:, 64:96]
        s16, r16 = vec(16), vec(16)
        mx, rsm = vec(2), vec(2)
        fb = vec(8)
        mag = vec(32)
        odd = vec(1)
        nbr = vec(8)

        def slot(t, i, n=1):
            return t[:, SL * i:SL * (i + n)]

        def ft(ap):
            return ap.rearrange("p (f t) -> p f t", t=T)

        def tok(ap, c=CH):
            return ap.rearrange("p (t c) -> p t c", c=c)

        X = tok(slot(W, 0, 4), D)
        XN = tok(slot(W, 4, 4), D)
        GB = slot(W, 8, 2)
        HB = [tok(slot(W, 4 + i)) for i in range(2)]
        M = tok(slot(W, 6, 4), D)
        TMP = [tok(slot(W, 10 + i)) for i in range(2)]
        ST = [tok(slot(W, i)) for i in range(2)]
        GT = [tok(slot(G, k)) for k in range(4)]

        def rows(name):
            return A[name][0].rearrange("(k p) n -> p k n", p=P)

        class Chunk:
            def __init__(self, w, col, nu, lhs, l0, by, tag):
                self.w, self.col, self.nu, self.lhs, self.l0, self.by, self.tag = w, col, nu, lhs, l0, by, tag

        w_in, w_in2 = rows("w_in"), rows("w_in_2")
        wo, wo2 = rows("w_out"), rows("w_out_2")
        wb = [A["w_branch"][0, k].rearrange("(k p) n -> p k n", p=P) for k in range(4)]
        wb2 = [A["w_branch_2"][0, k].rearrange("(k p) n -> p k n", p=P) for k in range(3)]
        wglu = rows("s5_w_glu_2")
        proj1 = [Chunk(w_in, c, 8, "X", 0, "act", (tag, 0)) for tag, c in (
            ("q", 2560), ("k", 3072), ("v", 3584), ("xa", 0), ("xp", 512), ("gc", 1536), ("xc", 2048), ("gb", 1024))]
        FCOL, GATE1, GATE2 = 4096, 4104, 6144

        def gates1(n):
            return [Chunk(w_in, GATE1 + D * k + CH * n, 8, "X", 0, "act", ("gate", n, k)) for k in range(4)]

        def prods1(n):
            return [Chunk(wb[k], CH * n, 2, "Y", 4 * k, "dve", ("prod", n, k)) for k in range(4)]

        proj2 = [Chunk(w_in2, base + CH * h, 8, "X", 0, "act", (tag, h)) for tag, base in (
            ("s5", 2048), ("q", 3072), ("k", 4096), ("v", 5120), ("gv", 1024), ("u", 0)) for h in range(2)]

        def gates2(n):
            return [Chunk(w_in2, GATE2 + D * k + CH * n, 8, "X", 0, "dve", ("gate", n, k)) for k in range(3)]

        def prods2(n):
            return [Chunk(wb2[k], CH * n, 4, "Y", 8 * k, "dve", ("prod", n, k)) for k in (2, 0, 1)]

        glu = [Chunk(wglu, CH * h, 4, "Y", 8, "act", ("glu", h)) for h in range(2)]

        def outs(w):
            return [Chunk(w, CH * n, 8, "X", 0, "dve", ("out", n)) for n in range(NCH)]

        plan = {(1, "a"): proj1 + gates1(0),
                (1, "b"): prods1(0) + sum((gates1(n) + prods1(n) for n in range(1, NCH)), []) + outs(wo),
                (2, "a"): proj2 + gates2(0),
                (2, "b"): glu + prods2(0) + sum((gates2(n) + prods2(n) for n in range(1, NCH)), []) + outs(wo2)}
        blocks = {"both": (1, 2), "first": (1,), "second": (2,)}[MODE]
        u0, ts0, down0, find = {}, {}, {}, {}
        u = ts = 0
        counts = {"act": 0, "dve": 0}
        chunks = []
        for b in blocks:
            for ph in "ab":
                u0[b, ph] = u
                for ch in plan[b, ph]:
                    counts[ch.by] += 1
                    ch.n, ch.u0, ch.evicted = len(chunks), u, counts[ch.by]
                    chunks.append(ch)
                    find[(b,) + ch.tag] = ch
                    u += ch.nu
            u0[b, "m"] = u
            u += NF * 16
            down0[b] = counts["dve"]
            counts["dve"] += NF * NCH
            chunks += [None] * (len(chunks) % 2)
            ts0[b] = ts
            ts += 24 + 2 * NF
        evict = {"act": S("acc_read_by_act"), "dve": S("acc_read_by_dve")}
        raw_in = [S(f"raw_in{i}") for i in range(RING)]
        hi_done, lo_done, used = S("whi_ready"), S("wlo_ready"), S("units_multiplied")
        ts_ready, ts_split = S("transposed"), S("transposes_split")
        NB = len(blocks)
        XS = [A["x"][0], A["x1"]]

        def gates_of(b):
            return 4 if b == 1 else 3

        def mlp_base(b, j):
            return j * 16 + (u0[b, "m"] + 8)

        def yready(b, k):
            return S(f"y{b}{k}_ready")

        QT1, KT1 = ft(slot(Z, 4)), ft(slot(Z, 5))
        PB = [slot(Z, 10)[:, 384 * i:384 * i + 384] for i in range(2)]
        PTB = [slot(Z, 11)[:, 384 * i:384 * i + 384] for i in range(2)]
        CUMT = slot(Z, 10)[0:8, 768:1024]
        LZ, LE, LH, LQ, LS = (slot(Z, 11)[:, 768 + 20 * i:788 + 20 * i] for i in range(5))
        Q1, K1, V1 = (tok(slot(W, i)) for i in (11, 12, 13))
        L_X, L_U, L_R, L_G, L_T, L_A = (ft(slot(W, i)) for i in (2, 3, 4, 5, 6, 7))
        P_X, P_P, P_Q = (ft(slot(W, i)) for i in (8, 9, 10))
        S_C, S_Y, S_B = (ft(slot(W, i)) for i in (11, 12, 2))
        BD = slot(G, 0).rearrange("p (w f c) -> p w f c", w=2, f=4)
        PW = slot(G, 1)[:, 0:512].rearrange("p (g j) -> p g j", g=4)
        SEL = slot(G, 2)[0:8, :].rearrange("p (h c) -> p h c", h=8)
        CNT = slot(G, 3)[:, 0:16]
        LRUQ, PMQ, HQ1 = [48, 57, 66, 75], [78, 81], 30
        XI, GS, SG = ft(slot(W, 2, 2)), ft(slot(W, 4, 2)), ft(slot(W, 2, 2))
        QT2, KT2 = ft(slot(W, 9, 2)), ft(slot(W, 11, 2))
        A_E, A_W = slot(W, 13)[:, 0:384], slot(W, 13)[:, 384:768]
        VT, GV, GU = tok(slot(Z, 0, 2), 1024), tok(slot(Z, 6, 2), 1024), tok(slot(W, 0, 2), 1024)
        GMG = slot(W, 6)
        BT = [slot(Z, 2 + r).rearrange("p (i c) -> p i c", i=8) for r in range(2)]
        CT = [slot(Z, 8 + r).rearrange("p (i c) -> p i c", i=8) for r in range(2)]
        GW = slot(G, 3).rearrange("p (g c) -> p g c", g=8)
        BPAD = [slot(W, 4 + r) for r in range(2)]
        CPAD = [slot(W, 9 + r) for r in range(2)]
        BSRC = slot(Z, 10).rearrange("p (r j h) -> p r j h", r=2, j=32)
        CSRC = slot(Z, 4).rearrange("p (r i q) -> p r i q", r=2, i=8)
        GWSRC = slot(Z, 6).rearrange("p (g s) -> p g s", g=8)
        PLO = slot(Z, 11)[:, 0:256].rearrange("p (r k j) -> p r k j", r=2, k=4)
        PHI = slot(W, 13)[:, 768:1024].rearrange("p (r k j) -> p r k j", r=2, k=4)
        D_S, D_C, D_N = (slot(Z, 5)[:, 288 * i:288 * i + 288] for i in range(3))
        D_DT, D_X, D_TH, D_R, D_I = (slot(Z, 5)[:, 864 + 32 * i:896 + 32 * i] for i in range(5))
        D_KR, D_KI, D_D, D_U, D_V = (slot(Z, 11)[:, 256 + 32 * i:288 + 32 * i] for i in range(5))
        BTMP = slot(Z, 11)[:, 512:1024]
        TAB = [slot(G, i).rearrange("p (r j l) -> p r j l", r=2, j=2) for i in range(2)]
        W16 = slot(G, 2).rearrange("p (r j l) -> p r j l", r=2, j=32)
        ROT = [slot(W, 7)[:, 512 * i:512 * i + 512].rearrange("p (r t) -> p r t", r=2) for i in range(2)]
        D1, D2 = (slot(W, 6)[:, 512 * i:512 * i + 512].rearrange("p (r t) -> p r t", r=2) for i in range(2))
        ST1, ST2 = slot(W, 8)[:, 0:512], slot(W, 8)[:, 512:1024]
        STATE = ST1.rearrange("p (r t) -> p r t", r=2)
        S5Q, HQ2, GQ = 26, 57, 104
        GLUQ = [8, 9, 12, 13]
        n_a = {b: u0[b, "b"] - u0[b, "a"] for b in blocks}
        BQ = [6 + 2 * n for n in range(10)]
        MT_SRC = [(m, i) for m in (CPAD[0], CPAD[1], BPAD[0], BPAD[1], slot(Z, 6)) for i in range(2)]
        MT_DST = [slot(m, j)[:, CH * i:CH * i + CH] for m, j in ((Z, 8), (Z, 9), (Z, 2), (Z, 3), (G, 3)) for i in range(2)]
        TP = {1: [(tag, t, q + 3 * t) for tag, q in (("q", 14), ("k", 22), ("xa", 34), ("xp", 42), ("gc", 51),
                                                     ("xc", 60), ("gb", 69)) for t in range(NT)],
              2: [((tag, h), t, 8 * c + 10 + 3 * t) for c, (tag, h) in enumerate(
                  (tg, hh) for tg in ("s5", "q", "k") for hh in range(2)) for t in range(NT)]}
        TDST = {1: {"q": QT1, "k": KT1, "xa": L_X, "xp": P_X, "gc": S_C, "xc": S_Y, "gb": S_B},
                2: {(tg, h): m[:, 4 * h:4 * h + 4, :] for tg, m in (("s5", XI), ("q", QT2), ("k", KT2)) for h in range(2)}}
        TBANK = {1: PU[1], 2: PT[0]}
        sbase = {1: 0, 2: len(TP[1]) if len(blocks) > 1 else 0}
        stage_base = {1: 4, 2: sbase[2]}
        YN = {(1, 0): 1, (1, 1): 1, (1, 2): 1, (1, 3): 4, (2, 0): 4, (2, 1): 1, (2, 2): 8}

        def bias_buf(n, k):
            if n == 0:
                return slot(W, 7, 2)[:, CH * k:CH * k + CH]
            return slot(W, 12)[:, CH * ((3 * n + k) % 2):CH * ((3 * n + k) % 2) + CH]

        def end_of(b, ch):
            return ch.u0 + ch.nu - u0[b, "a"]

        def merge_positions(b):
            p3 = find[(b, "prod", NCH - 1, 0 if b == 1 else 2)].u0 - u0[b, "a"]
            po = find[(b, "out", 0)].u0 - u0[b, "a"]
            return [p3 + 1 + i for i in range(6)] + [po - 1] * 2

        block = ctx.enter_context(nc.Block())

        @block.sync
        def _(sp_):
            def load(base, i, view):
                if not (isinstance(base, int) and base + i < RING):
                    sp_.wait_ge(lo_done, base + (i - RING + 1))
                sp_.dma_start(raw[:, i % RING, :].rearrange("p (k n) -> p k n", n=CH), view)\
                   .then_inc(raw_in[i % RING], 16)

            for b in blocks:
                for ph in "ab":
                    for ch in plan[b, ph]:
                        for i in range(ch.nu):
                            load(0, ch.u0 + i, ch.w[:, UK * i:UK * i + UK, ch.col:ch.col + CH])
                up = rows("w_mlp_up" if b == 1 else "w_mlp_in_2")
                dn = rows("w_mlp_down" if b == 1 else "w_mlp_out_2")
                for i in range(8):
                    load(0, u0[b, "m"] + i, up[:, UK * i:UK * i + UK, 0:CH])
                with sp_.Fori(0, NF - 1) as j:
                    for i in range(8):
                        load(mlp_base(b, j), i, up[:, UK * i:UK * i + UK, bass.ds(j * CH + CH, CH)])
                    for i in range(8):
                        n = i // 2
                        load(mlp_base(b, j), 8 + i, dn[:, bass.ds(j * 4 + UK * (i % 2), UK), CH * n:CH * n + CH])
                for i in range(8):
                    n, k = i // 2, 4 * (NF - 1) + UK * (i % 2)
                    load(mlp_base(b, NF - 1), i, dn[:, k:k + UK, CH * n:CH * n + CH])
            for t in range(NT):
                sp_.wait_ge(S("normed"), NT * 2 * NB + t + 1)
                sp_.dma_start(out[0, P * t:P * t + P, :], XN[:, t, :]).then_inc(S("out_written"), 16)
            sp_.wait_ge(S("out_written"), 16 * NT)

        @block.gpsimd
        def _(pool):
            count = [0]

            def chain(ins):
                count[0] += 1
                ins.then_inc(S("pool_chain"), 1)
                pool.wait_ge(S("pool_chain"), count[0])

            tt = nc.gpsimd.tensor_tensor
            gains = [A["norm_mix_g"][0], A["norm_mlp_g"][0], A["norm1_g_2"][0], A["norm2_g_2"][0]]
            gains = ({1: gains[:2], 2: gains[2:]}[blocks[0]] if NB == 1 else gains) + [A["final_g_2"]]

            def load_gain(m):
                pool.dma_start(GB, gains[m].partition_broadcast(P)).then_inc(S("gain_in"), 16)

            pool.dma_start(X, A["x"][0].rearrange("(t p) n -> p t n", p=P)).then_inc(S("x_in"), 16)
            load_gain(0)
            va, vb = slot(Z, 0)[:, 0:P], slot(Z, 0)[:, P:2 * P]
            ld = slot(Z, 0)[:, 2 * P:2 * P + 2]
            chain(nc.gpsimd.memset(va, 0.0))
            chain(nc.gpsimd.memset(va[96:128, :].rearrange("p (a b c) -> p a b c", b=2, c=16)[:, :, 0, :], 1.0))
            at = 0
            for name in ("lru_conv_w", "lru_conv_b", "lru_br", "lru_bi", "lru_lambda", "pool_scale", "sconv_w",
                         "s5_d_2", "s5_b_glu_2", "gm_b_s_2"):
                src = A[name][0]
                src = src.rearrange("(f p) -> f p", p=P) if len(src.shape) == 1 else \
                    src.rearrange("k (f p) -> (k f) p", p=P)
                n = src.shape[0]
                pool.dma_start(va[at:at + n, :], src).then_inc(S("vectors_in"), 16)
                at += n
            pool.dma_start(vb[0:32, :], A["s5_lambda_re_2"][0].rearrange("(j g) p -> j (g p)", g=2)).then_inc(S("vectors_in"), 16)
            pool.dma_start(vb[32:64, :], A["s5_lambda_im_2"][0].rearrange("(j g) p -> j (g p)", g=2)).then_inc(S("vectors_in"), 16)
            pool.dma_start(ld[64:96, :], A["s5_log_dt_2"][0].rearrange("(j g) -> j g", g=2)).then_inc(S("vectors_in"), 16)
            for m, v in ((ident, 0.0), (UP, 1.0), (NLOW, -1.0), (CM, 0.0), (SM, 0.0), (S01, 1.0)):
                chain(nc.gpsimd.memset(m[:, :], v))
            for m, op, fill, base, step, cm in (
                    (ident, ALU.not_equal, 1.0, 0, -1, 1), (UP, ALU.is_ge, 0.0, 0, 1, -1),
                    (NLOW, ALU.is_ge, 0.0, 0, -1, 1), (CM, ALU.is_ge, NEG, 0, -1, 1),
                    (SM, ALU.is_gt, NEG, 0, 1, -1), (S01, ALU.is_gt, 0.0, 0, 1, -1)):
                chain(nc.gpsimd.affine_select(out=m[:, :], in_=m[:, :], compare_op=op, fill=fill, base=base,
                                              pattern=[[step, m.shape[1]]], channel_multiplier=cm))
            nc.gpsimd.memset(NONE[:, :], -1.0).then_inc(S("masks_ready"), 1)

            def block1():
                pool.dma_start(wf[:, :, :], w_in[:, :, FCOL:FCOL + 8]).then_inc(S("small1_in"), 16)
                for i, name in enumerate(("q_norm_g", "k_norm_g")):
                    pool.dma_start(qg[:, i, :], A[name][0].partition_broadcast(P)).then_inc(S("small1_in"), 16)
                pool.dma_start(fb, A["forget_b"][0].partition_broadcast(P)).then_inc(S("small1_in"), 16)
                bd = BD
                chain(nc.gpsimd.memset(slot(G, 0), 0.0))
                for w, name in enumerate(("lru_wr", "lru_wi")):
                    for half in range(2):
                        pool.dma_start(bd[64 * half:64 * half + 64, w, :, 64 * half:64 * half + 64],
                                       A[name][0].rearrange("(f a) i j -> a i f j", a=2)[half]).then_inc(S("small1_in"), 16)
                pool.dma_start(slot(G, 1)[:, 0:512].rearrange("p (g j) -> p g j", g=4),
                               A["pool_w"][0].rearrange("g i j -> i g j")).then_inc(S("small1_in"), 16)
                sel = slot(G, 2)[0:8, :].rearrange("p (h c) -> p h c", h=8)
                chain(nc.gpsimd.memset(sel, 0.0))
                chain(nc.gpsimd.affine_select(out=sel, in_=sel, compare_op=ALU.not_equal, fill=-1.0, base=0,
                                              pattern=[[-1, 8], [0, P]], channel_multiplier=1))
                nc.gpsimd.iota(slot(G, 3)[:, 0:16], [[1, 16]], base=1, channel_multiplier=0,
                               allow_small_or_imprecise_dtypes=True).then_inc(S("sel_ready"), 1)

            def block2():
                pool.wait_ge(S("vA_ready"), 1)
                pool.wait_ge(used, u0[2, "a"])
                bsrc = BSRC
                for r, name in enumerate(("s5_b_re_2", "s5_b_im_2")):
                    pool.dma_start(bsrc[:, r], A[name][0].rearrange("(j g) p h -> (g p) j h", g=2)).then_inc(S("small2_in"), 16)
                csrc = CSRC
                for r, name in enumerate(("s5_c_re_2", "s5_c_im_2")):
                    pool.dma_start(csrc[:, r], A[name][0].rearrange("(i g) h q -> (g h) i q", i=8)).then_inc(S("small2_in"), 16)
                gw = GWSRC
                pool.dma_start(gw, A["gm_w_s_2"][0].rearrange("g t s -> t g s")).then_inc(S("small2_in"), 16)
                pool.wait_ge(S("small2_in"), 16 * 5)
                nc.gpsimd.affine_select(out=gw, in_=gw, compare_op=ALU.is_ge, fill=0.0, base=0,
                                        pattern=[[0, 8], [-1, P]], channel_multiplier=1).then_inc(S("gm_w_tril"), 1)
                pw, plo, w16 = PHI, PLO, W16
                pool.wait_ge(S("powers_ready"), 1)
                pa, pb = ST1, ST2

                def double(c, s, lo, nj, pc, ps, ta, tb, done=None):
                    ta = ta[:, 0:nj * lo].rearrange("p (j l) -> p j l", j=nj)
                    tb = tb[:, 0:nj * lo].rearrange("p (j l) -> p j l", j=nj)
                    pc = pc.unsqueeze(2).to_broadcast([P, nj, lo])
                    ps = ps.unsqueeze(2).to_broadcast([P, nj, lo])
                    c0, s0 = c[:, :, 0:lo], s[:, :, 0:lo]
                    tt(ta, c0, pc, ALU.mult)
                    chain(tt(tb, s0, ps, ALU.mult))
                    chain(tt(c[:, :, lo:2 * lo], ta, tb, ALU.subtract))
                    tt(ta, c0, ps, ALU.mult)
                    chain(tt(tb, s0, pc, ALU.mult))
                    if done is None:
                        chain(tt(s[:, :, lo:2 * lo], ta, tb, ALU.add))
                    else:
                        tt(s[:, :, lo:2 * lo], ta, tb, ALU.add).then_inc(S(done[0]), 1)
                        pool.wait_ge(S(done[0]), done[1])

                nc.gpsimd.memset(w16[:, 0, :, 0:1], 1.0)
                chain(nc.gpsimd.memset(w16[:, 1, :, 0:1], 0.0))
                for k in range(4):
                    double(w16[:, 0], w16[:, 1], 1 << k, 32, plo[:, 0, k], plo[:, 1, k], pa, pb)
                tabs, rr = TAB, ROT
                ps_, pq = (v.rearrange("p (r t) -> p r t", r=2) for v in (pa, pb))

                def tables(h):
                    tab = tabs[h % 2]
                    if h >= 2:
                        pool.wait_ge(S("s5_r_ready"), 2 * h - 2)
                    for r in range(2):
                        chain(nc.gpsimd.tensor_copy(tab[:, r, :, 0:16], w16[:, r, 2 * h:2 * h + 2, :]))
                    for k in range(4, 8):
                        double(tab[:, 0], tab[:, 1], 1 << k, 2, pw[:, 0, k - 4, 2 * h:2 * h + 2],
                               pw[:, 1, k - 4, 2 * h:2 * h + 2], pb[:, 0:256], pb[:, 256:512],
                               ("table_ready", h + 1) if k == 7 else None)

                def remod(j):
                    tab, r = tabs[(j // 2) % 2], rr[j % 2]
                    c = tab[:, 0, j % 2].unsqueeze(1).to_broadcast([P, 2, T])
                    s = tab[:, 1, j % 2].unsqueeze(1).to_broadcast([P, 2, T])
                    pool.wait_ge(S("s5_r_ready"), j + 1)
                    if j:
                        pool.wait_ge(S("s5_read"), j)
                    tt(ps_, r, c, ALU.mult)
                    chain(tt(pq, r, s, ALU.mult))
                    tt(ps_[:, 0], ps_[:, 0], pq[:, 1], ALU.subtract)
                    tt(ps_[:, 1], ps_[:, 1], pq[:, 0], ALU.add).then_inc(S("s5_state_ready"), 1)
                    pool.wait_ge(S("s5_state_ready"), j + 1)

                tables(0)
                for h in range(16):
                    if h + 1 < 16:
                        tables(h + 1)
                    remod(2 * h)
                    remod(2 * h + 1)
                pool.wait_ge(S("s5_read"), 32)
                pool.dma_start(GMG, A["gm_norm_g_2"][0].partition_broadcast(P)).then_inc(S("gm_gain_in"), 16)
                for k in range(3):
                    load_bias(0, k)

            def load_bias(n, k):
                pool.dma_start(bias_buf(n, k), A["b_gate_2"][0, k, CH * n:CH * n + CH].partition_broadcast(P))\
                    .then_inc(S(f"bias_in{k}"), 16)

            def load_biases(lo, hi):
                for i in range(lo, hi):
                    if i >= 5:
                        g = find[(2, "gate", (i - 2) // 3, (i - 2) % 3)]
                        pool.wait_ge(evict["dve"], g.evicted)
                    load_bias(i // 3, i % 3)

            added = 0
            for bi_, b in enumerate(blocks):
                (block1 if b == 1 else block2)()
                for k in range(gates_of(b)):
                    pool.wait_ge(yready(b, k), YN[b, k])
                if b == 2:
                    load_biases(3, 5)
                pool.dma_start(X, XS[bi_ if NB > 1 else 0].rearrange("(t p) n -> p t n", p=P)).then_inc(S("x_in"), 16)
                for n in range(NCH):
                    order = [0, 1, 2, 3] if b == 1 else [2, 0, 1]
                    m = M[:, :, CH * n:CH * n + CH]
                    for k in order[1:]:
                        added += 1
                        pool.wait_ge(evict["dve"], find[(b, "prod", n, k)].evicted)
                        tt(m, m, TMP[added % 2], ALU.add).then_inc(S("tmp_added"), 1)
                        pool.wait_ge(S("tmp_added"), added)
                    if b == 2 and n + 1 < NCH:
                        load_biases(3 * n + 5, min(3 * n + 8, 12))
                pool.wait_ge(ts_split, ts0[b] + 16)
                load_gain(2 * bi_ + 1)
                pool.wait_ge(S("normed"), NT * (2 * bi_ + 2))
                load_gain(2 * bi_ + 2)
                if b != blocks[-1]:
                    pool.wait_ge(evict["dve"], down0[b] + NF * NCH)
                    pool.dma_start(A["x1"].rearrange("(t p) n -> p t n", p=P), X).then_inc(S("x_saved"), 16)
                    pool.wait_ge(S("x_saved"), 16)

        @block.scalar
        def _(act):
            st = {"hi": 0, "ts": 0, "norm": 0, "n": 0}

            def chain(ins):
                st["n"] += 1
                ins.then_inc(S("act_chain"), 1)
                act.wait_ge(S("act_chain"), st["n"])

            def a(out_, in_, f=ACT.Copy, **kw):
                return nc.scalar.activation(out_, in_, f, **kw)

            def hi(base, i):
                act.wait_ge(raw_in[i % RING], base * 4 + (16 * (i // RING) + 16))
                if not (isinstance(base, int) and base + i < RING):
                    act.wait_ge(used, base + (i - RING + 1))
                a(whi[:, i % RING, :], raw[:, i % RING, :]).then_inc(hi_done, 1)

            def hi_upto(n):
                while st["hi"] < n:
                    hi(0, st["hi"])
                    st["hi"] += 1

            def norm_scale(need):
                m = st["norm"]
                st["norm"] += 1
                act.wait_ge(*need)
                for t in range(NT):
                    a(XN[:, t, :], X[:, t, :], ACT.Square, accum_out=ss[:, t:t + 1]).then_inc(S("squares"), 1)
                act.wait_ge(S("mean_square"), m + 1)
                a(rs, rs, ACT.Sqrt).then_inc(S("root"), 1)

            def staged(ch, dst, f=ACT.Copy, **kw):
                act.wait_ge(used, ch.u0 + ch.nu)
                for t in range(NT):
                    ins = a(dst[:, t, :], PA[ch.n % 2][t], f, **kw)
                ins.then_inc(evict["act"], 1)

            def evictions(b):
                stages = 0
                for ch in plan[b, "a"] + plan[b, "b"]:
                    tag, h = ch.tag[0], ch.tag[1]
                    if tag == "gate" and b == 2:
                        yield end_of(b, ch) + 4
                        act.wait_ge(evict["dve"], ch.evicted)
                        a(GT[ch.tag[2]], GT[ch.tag[2]], ACT.Sigmoid).then_inc(S("gates_ready2"), 1)
                        continue
                    if ch.by != "act":
                        continue
                    yield end_of(b, ch) + 3
                    if tag == "gate":
                        n, k = ch.tag[1:]
                        if n == 0:
                            act.wait_ge(S(("lru_mm", "pool_mm", "scored", "pool_done")[k]), (4, 2, 8, 1)[k])
                            staged(ch, GT[k])
                            if k == 3:
                                for kk in range(4):
                                    act.wait_ge(evict["act"], ch.evicted)
                                    a(GT[kk], GT[kk], ACT.Sigmoid).then_inc(S("gates_ready1"), 1)
                        else:
                            act.wait_ge(evict["dve"], find[(1, "prod", n - 1, k)].evicted)
                            staged(ch, GT[k], ACT.Sigmoid)
                    elif b == 1 and tag in "qkv":
                        staged(ch, {"q": Q1, "k": K1, "v": V1}[tag])
                    elif tag == "v":
                        staged(ch, VT[:, :, CH * h:CH * h + CH])
                    elif tag == "gv":
                        if h == 0:
                            act.wait_ge(S("s5_mT"), 10)
                        staged(ch, GV[:, :, CH * h:CH * h + CH], ACT.Gelu_apprx_tanh)
                    elif tag == "u":
                        if h == 0:
                            act.wait_ge(S("stage_transposed"), sbase[2] + len(TP[2]))
                        staged(ch, GU[:, :, CH * h:CH * h + CH], ACT.Gelu_apprx_tanh)
                    elif tag == "glu":
                        act.wait_ge(S("gm_T"), 4)
                        staged(ch, ST[h])
                    else:
                        if b != blocks[0] and stages == 0:
                            act.wait_ge(S("x_saved"), 16)
                        if stages >= 2:
                            act.wait_ge(S("stage_transposed"), stage_base[b] + 2 * (stages - 1))
                        staged(ch, ST[stages % 2])
                        stages += 1

            def copies(b):
                for n, (tag, t, q) in enumerate(TP[b]):
                    yield q + 2
                    act.wait_ge(S("stage_transposed"), sbase[b] + n + 1)
                    if tag == "gb":
                        act.wait_ge(S("lru_u"), 1)
                    scale = 128.0 ** -0.5 if tag[0] == "q" and b == 2 else 1.0
                    a(TDST[b][tag][:, :, P * t:P * t + P], TBANK[b].rearrange("p (f t) -> p f t", t=P),
                      scale=scale).then_inc(S("stage_copied"), 1)

            def lru():
                yield 1
                act.wait_ge(S("small1_in"), 16 * 9)
                a(wfh[:, :, :], wf[:, :, :]).then_inc(S("wf_hi"), 1)
                yield 9
                act.wait_ge(S("z_ready"), 1)
                chain(a(LE, LZ, ACT.Abs))
                a(LE, LE, ACT.Exp, scale=-1.0).then_inc(S("z_exp"), 1)
                yield 13
                act.wait_ge(S("cum_mm"), 1)
                a(CUMT, PU[1][0:8, 0:T]).then_inc(S("cumT_ready"), 1)
                for f in range(4):
                    yield LRUQ[f] + 2
                    act.wait_ge(S("lru_mm"), f + 1)
                    a(L_R[:, f, :], PU[1][:, 0:T], ACT.Exp, scale=-1.0, bias=nbr[:, f:f + 1])
                    a(L_G[:, f, :], PU[1][:, T:2 * T], ACT.Exp, scale=-1.0, bias=nbr[:, 4 + f:5 + f]).then_inc(S("lru_exp"), 1)
                yield LRUQ[3] + 3
                act.wait_ge(S("log_a"), 1)
                a(L_T, L_R, ACT.Tanh).then_inc(S("lru_tanh"), 1)
                a(L_A, L_R, ACT.Exp).then_inc(S("lru_a"), 1)
                yield LRUQ[3] + 6
                act.wait_ge(S("lru_1ma2"), 1)
                a(L_R, L_T, ACT.Sqrt).then_inc(S("lru_sqrt"), 1)
                yield LRUQ[3] + 12
                act.wait_ge(S("lru_h"), 1)
                a(YH[:, 0:4, :], L_U).then_inc(S("y_hi10"), 1)

            def pool_sconv():
                for h in range(2):
                    yield PMQ[h] + 2
                    act.wait_ge(S("pool_mm"), h + 1)
                    for g in range(2):
                        ins = a(P_P[:, 2 * h + g, :], PU[1][:, T * g:T * g + T], scale=pscale[:, 2 * h + g:2 * h + g + 1])
                    ins.then_inc(S("pool_scaled"), 1)
                act.wait_ge(S("pool_scaled"), 2)
                a(YH[:, 4:8, :], P_P).then_inc(S("y_hi11"), 1)
                yield 83
                act.wait_ge(S("sconv_ready"), 1)
                a(YH[:, 8:12, :], S_Y).then_inc(S("y_hi12"), 1)

            def attn1():
                yield 12
                for i in range(2):
                    yield 12 + 8 * i
                    act.wait_ge(S("qk_ms"), i + 1)
                    a(r16, s16, ACT.Sqrt).then_inc(S("qk_root"), 1)
                for h in range(8):
                    q0 = HQ1 + 5 * h
                    yield q0 + 2
                    act.wait_ge(S("row_max"), h + 1)
                    p_ = PB[h % 2]
                    if h >= 2:
                        act.wait_ge(S("p_transposed"), h - 1)
                    a(p_[:, 0:P], PU[0][:, 0:P], ACT.Exp, bias=mx[:, 0:1], accum_out=rsm[:, 0:1])
                    a(p_[:, P:3 * P], PU[0][:, P:3 * P], ACT.Exp, bias=mx[:, 1:2], accum_out=rsm[:, 1:2]).then_inc(S("p_exp"), 1)
                    yield q0 + 5
                    act.wait_ge(S("p_transposed"), h + 1)
                    if h >= 2:
                        act.wait_ge(S("attn_mm"), h - 1)
                    a(PTB[h % 2], PT[0][:, 0:3 * P]).then_inc(S("pT_ready"), 1)
                    if h % 2:
                        yield q0 + 8
                        act.wait_ge(S("attn_mm"), h + 1)
                        i = h // 2
                        a(YH[:, 12 + i, :], PT[1][:, T * (i % 2):T * (i % 2) + T]).then_inc(S("y_hi13"), 1)

            def s5a():
                yield 2
                a(D_DT, log_dt, ACT.Exp).then_inc(S("s5_dt"), 1)
                act.wait_ge(S("s5_x"), 1)
                a(D_TH, D_X, ACT.Tanh, scale=0.5)
                a(mag, D_X, ACT.Exp).then_inc(S("s5_mag"), 1)
                yield 3
                act.wait_ge(S("s5_reduced"), 1)
                a(D_C, D_S, ACT.Abs).then_inc(S("s5_abs"), 1)
                act.wait_ge(S("s5_cos_arg"), 1)
                a(D_C, D_C, ACT.Sin)
                a(D_S, D_S, ACT.Sin).then_inc(S("s5_sin"), 1)
                for n in range(10):
                    yield BQ[n] + 2
                    act.wait_ge(S("s5_mT"), n + 1)
                    a(MT_DST[n], PT[1]).then_inc(S("s5_mT_copied"), 1)
                yield S5Q + 74
                act.wait_ge(S("s5_y"), 8)
                a(GS, GS, ACT.Gelu_apprx_tanh).then_inc(S("s5_g"), 1)
                act.wait_ge(S("s5_g"), 1)
                a(YH[:, 8:16, :], GS).then_inc(S("s5_g_hi"), 1)

            def attn2():
                for h in range(8):
                    q0 = HQ2 + 6 * h
                    yield q0 + 2
                    act.wait_ge(S("z_mm"), h + 1)
                    if h:
                        act.wait_ge(S("tri_mm"), h)
                    chain(a(A_E, PT[0][:, 0:384], ACT.Abs))
                    chain(a(A_E, A_E, ACT.Exp, scale=-1.0))
                    a(A_E, A_E, ACT.Ln, bias=1.0).then_inc(S("ln_ready"), 1)
                    yield q0 + 5
                    act.wait_ge(S("tri_mm"), h + 1)
                    if h:
                        act.wait_ge(S("sb_mm"), h)
                    a(A_W, PT[0][:, 0:384], ACT.Exp).then_inc(S("sb_w"), 1)
                    yield q0 + 8
                    act.wait_ge(S("sb_mm"), h + 1)
                    a(YH[:, 16 + h, :], PT[1][:, T:2 * T]).then_inc(S("y_hi22"), 1)

            def gmlp():
                yield GQ - 5
                act.wait_ge(S("s5_bu_read"), 32)
                act.wait_ge(evict["act"], find[(2, "gv", 1)].evicted)
                for t in range(NT):
                    a(banks[:, 4:6, :], GV[:, t, :].rearrange("p (a c) -> p a c", a=2), ACT.Square,
                      accum_out=ss[:, t:t + 1]).then_inc(S("gm_squares"), 1)
                    act.wait_ge(S("gm_squares"), t + 1)
                yield GQ - 2
                act.wait_ge(S("gm_ms"), 1)
                a(rs, rs, ACT.Sqrt).then_inc(S("gm_root"), 1)
                for n in range(4):
                    yield GQ + 10 + 2 * n
                    act.wait_ge(S("gm_T"), n + 1)
                    if n == 0:
                        act.wait_ge(S("sb_mm"), 8)
                    a(YH[:, 2 * n:2 * n + 2, :], PU[n % 2].rearrange("p (k t) -> p k t", t=T)).then_inc(S("y_hi20"), 1)

            def glu_out():
                for i in range(4):
                    yield n_a[2] + GLUQ[i] + 2
                    act.wait_ge(S("glu_T"), i + 1)
                    for kk in range(2):
                        f = 2 * i + kk
                        ins = a(SG[:, f, :], PT[i % 2][:, T * kk:T * kk + T], ACT.Sigmoid, bias=b_glu[:, f:f + 1])
                    ins.then_inc(S("glu_sig"), 1)
                yield n_a[2] + 17
                act.wait_ge(S("glu_y"), 1)
                a(YH[:, 8:16, :], GS).then_inc(S("y_hi21"), 1)

            def merge_hi(b):
                for i, q in enumerate(merge_positions(b)):
                    yield q + (2 if i < 6 else 3)
                    split_hi(ts0[b] + 8 + i, XH[:, UK * i:UK * i + UK, :])

            def split_hi(q, dst):
                act.wait_ge(ts_ready, q + 1)
                a(dst, PT[q % 2].rearrange("p (k t) -> p k t", t=T)).then_inc(S("ts_hi"), 1)

            def mlp(b):
                H0 = ts0[b] + 24

                def split_pair(j, r):
                    act.wait_ge(ts_ready, j * 2 + (H0 + r + 1))
                    a(YH[:, UK * r:UK * r + UK, :], PT[r].rearrange("p (k t) -> p k t", t=T)).then_inc(S("ts_hi"), 1)

                def relu(base, n):
                    act.wait_ge(used, base + 8)
                    for t in range(NT):
                        ins = a(HB[0][:, t, :], PU[t], ACT.Relu)
                    ins.then_inc(S(f"relu{b}_ready"), 1)

                def body(j):
                    base = mlp_base(b, j)
                    for i in range(7):
                        hi(base, i)
                    split_pair(j, 0)
                    split_pair(j, 1)
                    for i in range(7, 12):
                        hi(base, i)
                    relu(base, j + 1)
                    for i in range(12, 16):
                        hi(base, i)

                hi_upto(u0[b, "m"] + 8)
                for i in range(4):
                    hi(mlp_base(b, 0), i)
                relu(u0[b, "m"], 0)
                base = mlp_base(b, 0)
                for i in range(4, 7):
                    hi(base, i)
                split_pair(0, 0)
                split_pair(0, 1)
                for i in range(7, 12):
                    hi(base, i)
                relu(base, 1)
                for i in range(12, 16):
                    hi(base, i)
                with act.Fori(1, NF - 1) as j:
                    body(j)
                base = mlp_base(b, NF - 1)
                for i in range(4):
                    hi(base, i)
                split_pair(NF - 1, 0)
                split_pair(NF - 1, 1)
                for i in range(4, 8):
                    hi(base, i)
                st["hi"] = base + 8

            for bi_, b in enumerate(blocks):
                hi_upto(u0[b, "a"] + RING)
                norm_scale((S("x_in"), 16) if bi_ == 0 else (evict["dve"], down0[blocks[0]] + NF * NCH))
                for i in range(8):
                    split_hi(ts0[b] + i, XH[:, UK * i:UK * i + UK, :])
                gens = [Steps(g) for g in ([evictions(b), copies(b)] + (
                    [attn1(), lru(), pool_sconv()] if b == 1 else [s5a(), attn2(), gmlp(), glu_out()]) + [merge_hi(b)])]
                for p_ in range(u0[b, "m"] - u0[b, "a"]):
                    hi_upto(u0[b, "a"] + p_ + 1)
                    for g in gens:
                        g.upto(p_)
                for g in gens:
                    g.upto(10 ** 6)
                hi_upto(u0[b, "m"] + RING)
                norm_scale((evict["dve"], find[(b, "out", NCH - 1)].evicted))
                for i in range(8):
                    split_hi(ts0[b] + 16 + i, XH[:, UK * i:UK * i + UK, :])
                mlp(b)
            norm_scale((evict["dve"], down0[blocks[-1]] + NF * NCH))

        @block.vector
        def _(dve):
            st = {"lo": 0, "norm": 0, "n": 0, "added": 0}
            tt, ts, stt = nc.vector.tensor_tensor, nc.vector.tensor_scalar, nc.vector.scalar_tensor_tensor

            def chain(ins):
                st["n"] += 1
                ins.then_inc(S("dve_chain"), 1)
                dve.wait_ge(S("dve_chain"), st["n"])

            def lo(base, i):
                dve.wait_ge(hi_done, base + (i + 1))
                tt(wlo[:, i % RING, :], raw[:, i % RING, :], whi[:, i % RING, :].bitcast(F32), ALU.subtract)\
                    .then_inc(lo_done, 1)

            def lo_upto(n):
                while st["lo"] < n:
                    lo(0, st["lo"])
                    st["lo"] += 1

            def split_lo(q, r, hi_, dst):
                dve.wait_ge(S("ts_hi"), q + 1)
                tt(dst, PT[r].rearrange("p (k t) -> p k t", t=T), hi_.bitcast(F32), ALU.subtract).then_inc(ts_split, 1)

            def norm():
                m = st["norm"]
                st["norm"] += 1
                dve.wait_ge(S("squares"), NT * (m + 1))
                ts(rs, ss, 1.0 / D, EPS, ALU.mult, ALU.add).then_inc(S("mean_square"), 1)
                dve.wait_ge(S("root"), m + 1)
                chain(nc.vector.reciprocal(rs, rs))
                dve.wait_ge(S("gain_in"), 16 * (m + 1))
                for t in range(NT):
                    stt(XN[:, t, :], X[:, t, :], rs[:, t:t + 1], GB, ALU.mult, ALU.mult).then_inc(S("normed"), 1)

            def evictions(b):
                order = [0, 1, 2, 3] if b == 1 else [2, 0, 1]
                for ch in plan[b, "a"] + plan[b, "b"]:
                    if ch.by != "dve":
                        continue
                    acc = PA[ch.n % 2]
                    if ch.tag[0] == "gate":
                        yield end_of(b, ch) + 3
                        n, k = ch.tag[1:]
                        dve.wait_ge(used, ch.u0 + ch.nu)
                        dve.wait_ge(S(f"bias_in{k}"), 16 * (n + 1))
                        if n == 0:
                            dve.wait_ge(S("s5_state_ready"), 32)
                        for t in range(NT):
                            ins = tt(GT[k][:, t, :], acc[t], bias_buf(n, k), ALU.add)
                    elif ch.tag[0] == "prod":
                        yield end_of(b, ch) + 2
                        n, k = ch.tag[1:]
                        dve.wait_ge(used, ch.u0 + ch.nu)
                        if b == 1 and n > 0:
                            dve.wait_ge(evict["act"], find[(1, "gate", n, k)].evicted)
                        else:
                            dve.wait_ge(S(f"gates_ready{b}"), (4 if b == 1 else 3) * n + k + 1)
                        if k == order[0]:
                            dst = M[:, :, CH * n:CH * n + CH]
                        else:
                            st["added"] += 1
                            dst = TMP[st["added"] % 2]
                            if st["added"] > 2:
                                dve.wait_ge(S("tmp_added"), st["added"] - 2)
                        for t in range(NT):
                            ins = tt(dst[:, t, :], acc[t], GT[k][:, t, :], ALU.mult)
                    else:
                        yield end_of(b, ch) + 3
                        n = ch.tag[1]
                        dve.wait_ge(used, ch.u0 + ch.nu)
                        dve.wait_ge(S("x_in"), 16 * (blocks.index(b) + 2))
                        for t in range(NT):
                            x = X[:, t, CH * n:CH * n + CH]
                            ins = tt(x, acc[t], x, ALU.add)
                    ins.then_inc(evict["dve"], 1)

            def merge_lo(b):
                for i, q in enumerate(merge_positions(b)):
                    yield q + (2 if i < 6 else 3)
                    split_lo(ts0[b] + 8 + i, i % 2, XH[:, UK * i:UK * i + UK, :], XL[:, UK * i:UK * i + UK, :])

            def y_lo(b, k, kt, n, src, hi_count):
                dve.wait_ge(S(f"y_hi{b}{k}"), hi_count)
                tt(YL[:, kt:kt + n, :], src, YH[:, kt:kt + n, :].bitcast(F32), ALU.subtract).then_inc(yready(b, k), 1)

            def lru():
                yield 6
                dve.wait_ge(S("wf_hi"), 1)
                tt(wfl[:, :, :], wf[:, :, :], wfh[:, :, :].bitcast(F32), ALU.subtract).then_inc(S("wf_split"), 1)
                yield 9
                dve.wait_ge(S("f_mm"), 1)
                dve.wait_ge(S("vA_ready"), 1)
                tt(LZ[:, 0:16].rearrange("p (t h) -> p t h", t=2), PU[1][:, 0:16].rearrange("p (t h) -> p t h", t=2),
                   fb.unsqueeze(1).to_broadcast([P, 2, 8]), ALU.add)
                ts(nbr, vA[:, 20:28], -1.0, None, ALU.mult)
                nc.vector.tensor_copy(LZ[:, 16:20], lam).then_inc(S("z_ready"), 1)
                yield 10
                dve.wait_ge(S("z_exp"), 1)
                chain(ts(LH, LE, 2.0, None, ALU.add))
                chain(nc.vector.reciprocal(LH, LH))
                chain(tt(LE, LE, LH, ALU.mult))
                chain(tt(LQ, LE, LE, ALU.mult))
                chain(ts(LH, LQ, 2.0 / 17, None, ALU.mult))
                for c in (15, 13, 11, 9, 7, 5, 3):
                    chain(stt(LH, LH, 2.0 / c, LQ, ALU.add, ALU.mult))
                chain(stt(LH, LH, 2.0, LE, ALU.add, ALU.mult))
                chain(stt(LS, LZ, 0.0, LH, ALU.min, ALU.subtract))
                ts(LS[:, 16:20], LS[:, 16:20], 8.0, None, ALU.mult).then_inc(S("log_f"), 1)
                for f in range(4):
                    yield 40 + f
                    dve.wait_ge(S("stage_copied"), 6)
                    x, u_ = L_X[:, f, :], L_U[:, f, :]
                    chain(ts(u_, x, conv_w[:, 12 + f:13 + f], conv_b[:, f:f + 1], ALU.mult, ALU.add))
                    for k in (2, 1, 0):
                        s = 3 - k
                        ins = stt(u_[:, s:T], x[:, 0:T - s], conv_w[:, 4 * k + f:4 * k + f + 1], u_[:, s:T], ALU.mult, ALU.add)
                        if k or f < 3:
                            chain(ins)
                ins.then_inc(S("lru_u"), 1)
                yield LRUQ[3] + 2
                dve.wait_ge(S("lru_exp"), 4)
                chain(ts(L_R, L_R, 1.0, None, ALU.add))
                chain(nc.vector.reciprocal(L_R, L_R))
                for f in range(4):
                    ins = ts(L_R[:, f, :], L_R[:, f, :], LS[:, 16 + f:17 + f], None, ALU.mult)
                ins.then_inc(S("log_a"), 1)
                yield LRUQ[3] + 3
                chain(ts(L_G, L_G, 1.0, None, ALU.add))
                chain(nc.vector.reciprocal(L_G, L_G))
                yield LRUQ[3] + 4
                chain(tt(L_G, L_G, L_U, ALU.mult))
                yield LRUQ[3] + 5
                dve.wait_ge(S("lru_a"), 1)
                chain(tt(L_U, L_A, L_A, ALU.mult))
                chain(stt(L_T, L_U, 1.0, L_T, ALU.add, ALU.mult))
                ts(L_T, L_T, -1.0, 1.3e-35, ALU.mult, ALU.max).then_inc(S("lru_1ma2"), 1)
                yield LRUQ[3] + 7
                dve.wait_ge(S("lru_sqrt"), 1)
                chain(tt(L_G, L_G, L_R, ALU.mult))
                for f in range(4):
                    yield LRUQ[3] + 8 + f
                    ins = nc.vector.tensor_tensor_scan(L_U[:, f, :], L_A[:, f, :], L_G[:, f, :], 0.0, ALU.mult, ALU.add)
                ins.then_inc(S("lru_h"), 1)
                yield LRUQ[3] + 13
                y_lo(1, 0, 0, 4, L_U, 1)

            def pool():
                yield 48
                dve.wait_ge(S("sel_ready"), 1)
                chain(nc.vector.reciprocal(CNT, CNT))
                dve.wait_ge(S("stage_copied"), 8)
                src, dst = P_X, P_P
                for i, s in enumerate((1, 2, 4, 8)):
                    yield 49 + i
                    nc.vector.tensor_copy(dst[:, i:4, 0:s], src[:, i:4, 0:s])
                    chain(tt(dst[:, i:4, s:T], src[:, i:4, s:T], src[:, i:4, 0:T - s], ALU.add))
                    src, dst = dst, (P_Q if dst is P_P else P_P)
                for g in range(4):
                    yield 53 + g
                    win = 2 << g
                    w_ = (P_P if g % 2 == 0 else P_Q)[:, g, :]
                    chain(tt(w_[:, 0:win - 1], w_[:, 0:win - 1], CNT[:, 0:win - 1], ALU.mult))
                    x = P_X[:, g, :]
                    tt(x[:, 0:win - 1], w_[:, 0:win - 1], x[:, 0:win - 1], ALU.subtract)
                    ins = stt(x[:, win - 1:T], w_[:, win - 1:T], 1.0 / win, x[:, win - 1:T], ALU.mult, ALU.subtract)
                ins.then_inc(S("pool_done"), 1)
                yield PMQ[1] + 4
                y_lo(1, 1, 4, 4, P_P, 1)

            def sconv():
                yield 66
                dve.wait_ge(S("stage_copied"), 12)
                chain(tt(S_C, S_C, S_Y, ALU.mult))
                for f in range(4):
                    yield 67 + f
                    x, y = S_C[:, f, :], S_Y[:, f, :]
                    chain(ts(y, x, sconv_w[:, 8 + f:9 + f], None, ALU.mult))
                    for k in (1, 0):
                        s = 2 - k
                        chain(stt(y[:, s:T], x[:, 0:T - s], sconv_w[:, 4 * k + f:4 * k + f + 1], y[:, s:T], ALU.mult, ALU.add))
                yield 75
                dve.wait_ge(S("stage_copied"), 14)
                tt(S_Y, S_Y, S_B, ALU.mult).then_inc(S("sconv_ready"), 1)
                yield 85
                y_lo(1, 2, 8, 4, S_Y, 1)

            def attn1():
                for i, (m, f) in enumerate(((Q1, 1.0 / 8), (K1, 1.0))):
                    yield 12 + 8 * i
                    c = plan[1, "a"][i]
                    dve.wait_ge(evict["act"], c.evicted)
                    flat = slot(W, 11 + i).rearrange("p (g e) -> p g e", e=64)
                    sq = slot(W, 3)
                    chain(tt(sq, slot(W, 11 + i), slot(W, 11 + i), ALU.mult))
                    chain(nc.vector.tensor_reduce(s16, sq.rearrange("p (g e) -> p g e", e=64), AX, ALU.add))
                    ts(s16, s16, 1.0 / 64, EPS, ALU.mult, ALU.add).then_inc(S("qk_ms"), 1)
                    dve.wait_ge(S("qk_root"), i + 1)
                    chain(nc.vector.reciprocal(r16, r16))
                    if i == 0:
                        chain(ts(r16, r16, f, None, ALU.mult))
                    yield 13 + 8 * i
                    chain(tt(flat, flat, r16.unsqueeze(2).to_broadcast([P, 16, 64]), ALU.mult))
                    tt(flat, flat, qg[:, i, :].unsqueeze(1).to_broadcast([P, 16, 64]), ALU.mult).then_inc(S("qk_normed"), 1)
                for h in range(8):
                    q0 = HQ1 + 5 * h
                    yield q0 + 2
                    dve.wait_ge(S("scored"), h + 1)
                    if h:
                        dve.wait_ge(S("p_exp"), h)
                    nc.vector.tensor_reduce(mx[:, 0:1], PU[0][:, 0:P], AX, ALU.max)
                    chain(nc.vector.tensor_reduce(mx[:, 1:2], PU[0][:, P:3 * P], AX, ALU.max))
                    ts(mx, mx, -1.0, None, ALU.mult).then_inc(S("row_max"), 1)
                    yield q0 + 3
                    dve.wait_ge(S("p_exp"), h + 1)
                    p_ = PB[h % 2]
                    chain(nc.vector.reciprocal(rsm, rsm))
                    ts(p_[:, 0:P], p_[:, 0:P], rsm[:, 0:1], None, ALU.mult)
                    ts(p_[:, P:3 * P], p_[:, P:3 * P], rsm[:, 1:2], None, ALU.mult).then_inc(S("p_ready"), 1)
                    if h % 2:
                        yield q0 + 8
                        i = h // 2
                        y_lo(1, 3, 12 + i, 1, PT[1][:, T * (i % 2):T * (i % 2) + T].unsqueeze(1), i + 1)

            def s5():
                dve.wait_ge(S("vA_ready"), 1)
                yield 1
                dve.wait_ge(S("small2_in"), 16 * 5)
                for r in range(2):
                    sgn = 1.0 if r == 0 else -1.0
                    for q in range(2):
                        v = CPAD[r].rearrange("p (i q e) -> p i q e", i=8, q=2)[:, :, q, :]
                        ins = ts(v, CSRC[:, r], (even, odd)[q], sgn, ALU.mult, ALU.mult)
                ins.then_inc(S("c_pad"), 1)
                yield 2
                dve.wait_ge(S("s5_dt"), 1)
                tt(D_X, lam_re, D_DT, ALU.mult).then_inc(S("s5_x"), 1)
                chain(tt(D_C[:, 32:64], lam_im, D_DT, ALU.mult))
                for k in range(8):
                    ts(D_S[:, 32 * k + 32:32 * k + 64], D_C[:, 32:64], float(1 << k), None, ALU.mult)
                chain(ts(D_S[:, 0:32], D_C[:, 32:64], 0.5, None, ALU.mult))
                magic = 1.5 * 2.0 ** 23
                chain(ts(D_N, D_S, 0.15915494309189535, magic, ALU.mult, ALU.add))
                chain(ts(D_N, D_N, magic, None, ALU.subtract))
                for c in (6.28125, 1.934051513671875e-3, 1.2556658656e-06):
                    chain(stt(D_S, D_N, -c, D_S, ALU.mult, ALU.add))
                ts(D_S, D_S, 3.1415925, -3.1415925, ALU.min, ALU.max).then_inc(S("s5_reduced"), 1)
                yield 3
                dve.wait_ge(S("s5_abs"), 1)
                ts(D_C, D_C, -1.0, 1.5707963705062866, ALU.mult, ALU.add).then_inc(S("s5_cos_arg"), 1)
                yield 4
                dve.wait_ge(S("s5_sin"), 1)
                for r, m in enumerate((D_C, D_S)):
                    nc.vector.tensor_copy(PLO[:, r], m[:, 32:160].rearrange("p (k j) -> p k j", k=4))
                    ins = nc.vector.tensor_copy(PHI[:, r], m[:, 160:288].rearrange("p (k j) -> p k j", k=4))
                ins.then_inc(S("powers_ready"), 1)
                dve.wait_ge(S("s5_mag"), 1)
                cs, sn, sh = D_C[:, 32:64], D_S[:, 32:64], D_S[:, 0:32]
                chain(stt(D_R, mag, 1.0, D_TH, ALU.add, ALU.mult))
                chain(tt(D_R, D_R, cs, ALU.mult))
                chain(tt(D_U, sh, sh, ALU.mult))
                chain(stt(D_R, D_U, -2.0, D_R, ALU.mult, ALU.add))
                tt(D_I, mag, sn, ALU.mult)
                tt(D_U, lam_re, lam_re, ALU.mult)
                chain(tt(D_V, lam_im, lam_im, ALU.mult))
                chain(tt(D_D, D_U, D_V, ALU.add))
                chain(nc.vector.reciprocal(D_D, D_D))
                for dst, p, q, op in ((D_KR, D_R, D_I, ALU.add), (D_KI, D_I, D_R, ALU.subtract)):
                    tt(D_U, p, lam_re, ALU.mult)
                    chain(tt(D_V, q, lam_im, ALU.mult))
                    chain(tt(D_U, D_U, D_V, op))
                    chain(tt(dst, D_U, D_D, ALU.mult))
                yield 5
                def mul(dst, kk, r):
                    return tt(dst, BSRC[:, r], kk.unsqueeze(2).to_broadcast([P, 32, 16]), ALU.mult)
                b3 = BTMP.rearrange("p (j h) -> p j h", j=32)
                acc3 = slot(W, 6)[:, 0:512].rearrange("p (j h) -> p j h", j=32)
                for r in range(2):
                    chain(nc.vector.memset(BPAD[r], 0.0))
                    chain(mul(acc3, D_KR, r))
                    chain(mul(b3, D_KI, 1 - r))
                    chain(tt(acc3, acc3, b3, ALU.subtract if r == 0 else ALU.add))
                    pad = BPAD[r].rearrange("p (j q h) -> p j q h", j=32, q=2)
                    for q in range(2):
                        ins = nc.vector.tensor_copy(pad[64 * q:64 * q + 64, :, q, :], acc3[64 * q:64 * q + 64])
                    if r:
                        ins.then_inc(S("b_pad"), 1)
                    else:
                        chain(ins)
                for j in range(32):
                    if j >= 7 and j % 4 == 3:
                        yield S5Q + 2 * j + 1
                        skip(j // 4 - 1)
                    yield S5Q + 2 * j + 2
                    tab = TAB[(j // 2) % 2]
                    c = tab[:, 0, j % 2].unsqueeze(1).to_broadcast([P, 2, T])
                    s = tab[:, 1, j % 2].unsqueeze(1).to_broadcast([P, 2, T])
                    bu = PU[j % 2].rearrange("p (r t) -> p r t", r=2)
                    dve.wait_ge(S("bu_mm"), j + 1)
                    dve.wait_ge(S("table_ready"), j // 2 + 1)
                    tt(D1, bu, c, ALU.mult)
                    tt(D2, bu, s, ALU.mult).then_inc(S("s5_bu_read"), 1)
                    dve.wait_ge(S("s5_bu_read"), j + 1)
                    tt(D1[:, 0], D1[:, 0], D2[:, 1], ALU.add)
                    chain(tt(D1[:, 1], D1[:, 1], D2[:, 0], ALU.subtract))
                    if j >= 2:
                        dve.wait_ge(S("s5_state_ready"), j - 1)
                    m = mag[:, j:j + 1].to_broadcast([P, T])
                    nc.vector.tensor_tensor_scan(ROT[j % 2][:, 0], m, D1[:, 0], 0.0, ALU.mult, ALU.add)
                    nc.vector.tensor_tensor_scan(ROT[j % 2][:, 1], m, D1[:, 1], 0.0, ALU.mult, ALU.add).then_inc(S("s5_r_ready"), 1)
                    dve.wait_ge(S("s5_r_ready"), j + 1)
                yield S5Q + 72
                skip(7)

            def skip(i):
                dve.wait_ge(S("s5_read"), 4 * i + 4)
                stt(GS[:, i, :], XI[:, i, :], s5_d[:, i:i + 1], PT[1][:, 0:T], ALU.mult, ALU.add).then_inc(S("s5_y"), 1)

            def attn2():
                for h in range(8):
                    q0 = HQ2 + 6 * h
                    yield q0 + 2
                    dve.wait_ge(S("ln_ready"), h + 1)
                    chain(stt(A_E, PT[0][:, 0:384], 0.0, A_E, ALU.max, ALU.add))
                    tt(A_E[:, 0:P], A_E[:, 0:P], S01[:, :], ALU.mult)
                    tt(A_E[:, 2 * P:3 * P], A_E[:, 2 * P:3 * P], S01[:, :], ALU.mult).then_inc(S("sp_ready"), 1)
                    yield q0 + 8
                    y_lo(2, 2, 16 + h, 1, PT[1][:, T:2 * T].unsqueeze(1), h + 1)

            def gmlp():
                yield S5Q + 75
                dve.wait_ge(S("s5_g_hi"), 1)
                tt(YL[:, 8:16, :], GS, YH[:, 8:16, :].bitcast(F32), ALU.subtract).then_inc(S("s5_g_split"), 1)
                yield GQ - 3
                dve.wait_ge(S("gm_squares"), 2)
                ts(rs, ss, 1.0 / 1024, EPS, ALU.mult, ALU.add).then_inc(S("gm_ms"), 1)
                yield GQ - 2
                dve.wait_ge(S("gm_root"), 1)
                chain(nc.vector.reciprocal(rs, rs))
                dve.wait_ge(S("gm_gain_in"), 16)
                for t in range(NT):
                    yield GQ - 1 + t
                    stt(GV[:, t, :], GV[:, t, :], rs[:, t:t + 1], GMG, ALU.mult, ALU.mult).then_inc(S("gm_normed"), 1)
                for n in range(4):
                    yield GQ + 2 * n + 2
                    t, g0 = n // 2, 4 * (n % 2)
                    dve.wait_ge(S("gm_mixed"), n + 1)
                    dve.wait_ge(evict["act"], find[(2, "u", 1)].evicted)
                    for g in range(4):
                        uu = GU[:, t, P * (g0 + g):P * (g0 + g) + P]
                        ins = stt(uu, PU[n % 2][:, P * g:P * g + P], gm_b[:, g0 + g:g0 + g + 1], uu, ALU.add, ALU.mult)
                    ins.then_inc(S("gm_y"), 1)
                for n in range(4):
                    yield GQ + 10 + 2 * n
                    y_lo(2, 0, 2 * n, 2, PU[n % 2].rearrange("p (k t) -> p k t", t=T), n + 1)

            def glu_out():
                yield n_a[2] + 16
                dve.wait_ge(S("glu_sig"), 4)
                tt(GS, GS, SG, ALU.mult).then_inc(S("glu_y"), 1)
                yield n_a[2] + 18
                y_lo(2, 1, 8, 8, GS, 1)

            def mlp(b):
                H0, base_evict = ts0[b] + 24, down0[b]

                def square(n):
                    dve.wait_ge(S(f"relu{b}_ready"), n + 1)
                    tt(HB[1], HB[0], HB[0], ALU.mult).then_inc(S(f"hidden{b}_ready"), 1)

                def add(base, n):
                    dve.wait_ge(used, base + (8 + 2 * n + 2))
                    for t in range(NT):
                        x = X[:, t, CH * n:CH * n + CH]
                        ins = tt(x, PA[n % 2][t], x, ALU.add)
                    ins.then_inc(evict["dve"], 1)

                def split_pair(j, r):
                    split_lo(j * 2 + (H0 + r), r, YH[:, UK * r:UK * r + UK, :], YL[:, UK * r:UK * r + UK, :])

                def body(j, first):
                    base, last = mlp_base(b, j), mlp_base(b, j - 1)
                    lo(base, 0)
                    lo(base, 1)
                    if not first:
                        add(last, 2)
                    lo(base, 2)
                    lo(base, 3)
                    if first:
                        square(0)
                    else:
                        add(last, 3)
                    for i in range(4, 7):
                        lo(base, i)
                    split_pair(j, 0)
                    split_pair(j, 1)
                    for i in range(7, 12):
                        lo(base, i)
                    square(j + 1)
                    lo(base, 12)
                    lo(base, 13)
                    add(base, 0)
                    lo(base, 14)
                    lo(base, 15)
                    add(base, 1)

                lo_upto(u0[b, "m"] + 8)
                body(0, True)
                with dve.Fori(1, NF - 1) as j:
                    body(j, False)
                base, last = mlp_base(b, NF - 1), mlp_base(b, NF - 2)
                lo(base, 0)
                lo(base, 1)
                add(last, 2)
                lo(base, 2)
                lo(base, 3)
                add(last, 3)
                split_pair(NF - 1, 0)
                split_pair(NF - 1, 1)
                for i in range(4, 8):
                    lo(base, i)
                for n in range(NCH):
                    add(base - 8, n)
                st["lo"] = base + 8

            dve.wait_ge(S("vectors_in"), 16 * 13)
            vb3 = slot(Z, 0)[64:96, P:2 * P].rearrange("p (g e) -> p g e", g=2)
            nc.vector.tensor_copy(vb3, slot(Z, 0)[64:96, 2 * P:2 * P + 2].unsqueeze(2).to_broadcast([32, 2, 64]))\
                .then_inc(S("dt_rows"), 1)
            dve.wait_ge(S("vectors_mm"), 1)
            chain(nc.vector.tensor_copy(vA, PT[0][:, 0:P]))
            nc.vector.tensor_copy(vB, PT[0][:, P:P + 96])
            ts(odd, even, -1.0, 1.0, ALU.mult, ALU.add).then_inc(S("vA_ready"), 1)
            dve.wait_ge(S("vA_ready"), 1)
            for b in blocks:
                lo_upto(u0[b, "a"] + RING)
                norm()
                for i in range(8):
                    split_lo(ts0[b] + i, i % 2, XH[:, UK * i:UK * i + UK, :], XL[:, UK * i:UK * i + UK, :])
                gens = [Steps(g) for g in ([evictions(b)] + (
                    [attn1(), lru(), pool(), sconv()] if b == 1 else [s5(), attn2(), gmlp(), glu_out()]) + [merge_lo(b)])]
                for p_ in range(u0[b, "m"] - u0[b, "a"]):
                    lo_upto(u0[b, "a"] + p_ + 1)
                    for g in gens:
                        g.upto(p_)
                lo_upto(u0[b, "m"] + RING - 1)
                for g in gens:
                    g.upto(10 ** 6)
                lo_upto(u0[b, "m"] + RING)
                norm()
                for i in range(8):
                    split_lo(ts0[b] + 16 + i, i % 2, XH[:, UK * i:UK * i + UK, :], XL[:, UK * i:UK * i + UK, :])
                mlp(b)
            norm()

        @block.tensor
        def _(pe):
            st = {"norm": 0, "sb": 0, "s5_out": 0}

            def mm(out_, l, r, start=True, stop=True, **kw):
                return nc.tensor.matmul(out_, l, r, start=start, stop=stop, **kw)

            def tr(out_, in_):
                return nc.tensor.transpose(out_, in_, ident[:, :])

            def unit(base, i, lh, ll, kt, acc, first, last):
                pe.wait_ge(lo_done, base + (i + 1))
                for k in range(UK):
                    for t in range(NT):
                        for n, (l, w) in enumerate(((lh, whi), (lh, wlo), (ll, whi))):
                            ins = mm(acc[t], l[:, kt + k, P * t:P * t + P], w[:, i % RING, CH * k:CH * k + CH],
                                     start=first and k == 0 and n == 0, stop=last and k == UK - 1 and n == 2)
                ins.then_inc(used, 1)

            def pair(q, r, src, c0):
                for k in range(UK):
                    for t in range(NT):
                        ins = tr(PT[r][:, T * k + P * t:T * k + P * t + P], src[:, t, c0 + P * k:c0 + P * k + P])
                ins.then_inc(ts_ready, 1)

            def norm(first):
                st["norm"] += 1
                pe.wait_ge(S("normed"), NT * st["norm"])
                for i in range(8):
                    if first + i >= 2:
                        pe.wait_ge(ts_split, first + i - 1)
                    pair(first + i, i % 2, XN, 2 * P * i)
                pe.wait_ge(ts_split, first + 8)

            def stage_transposes(b):
                stages = 0
                for n, (tag, t, q) in enumerate(TP[b]):
                    yield q
                    if b == 1 and tag in "qk":
                        src = {"q": Q1, "k": K1}[tag]
                        pe.wait_ge(S("qk_normed"), 1 if tag == "q" else 2)
                    else:
                        src = ST[stages // 2 % 2]
                        pe.wait_ge(evict["act"], find[(b, tag, 0) if b == 1 else (b,) + tag].evicted)
                        stages += 1
                    if sbase[b] + n > 0:
                        pe.wait_ge(S("stage_copied"), sbase[b] + n)
                    if b == 1:
                        if n == 0:
                            pe.wait_ge(S("cumT_ready"), 1)
                        before = sum(lq < q for lq in LRUQ)
                        if before:
                            pe.wait_ge(S("lru_exp"), before)
                    for f in range(4):
                        ins = tr(TBANK[b][:, P * f:P * f + P], src[:, t, P * f:P * f + P])
                    ins.then_inc(S("stage_transposed"), 1)

            def lru():
                yield 7
                pe.wait_ge(S("wf_split"), 1)
                for t in range(NT):
                    for k in range(KD):
                        for n, (l, w) in enumerate(((XH, wfh), (XH, wfl), (XL, wfh))):
                            ins = mm(PU[1][:, 8 * t:8 * t + 8], l[:, k, P * t:P * t + P], w[:, k, :],
                                     start=k == 0 and n == 0, stop=k == KD - 1 and n == 2)
                ins.then_inc(S("f_mm"), 1)
                yield 11
                pe.wait_ge(S("log_f"), 1)
                pe.wait_ge(S("masks_ready"), 1)
                mm(PU[1][0:8, 0:T], LS[:, 0:8], UP[:, :])
                mm(PU[1][0:8, P:T], LS[:, 8:16], UP[:, 0:P], start=False, skip_group_check=True).then_inc(S("cum_mm"), 1)
                for f in range(4):
                    yield LRUQ[f]
                    pe.wait_ge(S("lru_u"), 1)
                    pe.wait_ge(S("small1_in"), 16 * 9)
                    pe.wait_ge(S("stage_copied"), sum(q < LRUQ[f] for _, _, q in TP[1]))
                    for w in range(2):
                        ins = mm(PU[1][:, T * w:T * w + T], BD[:, w, f, :], L_U[:, f, :])
                    ins.then_inc(S("lru_mm"), 1)
                for h in range(2):
                    yield PMQ[h]
                    pe.wait_ge(S("pool_done"), 1)
                    pe.wait_ge(S("lru_exp"), 4)
                    if h:
                        pe.wait_ge(S("pool_scaled"), 1)
                    for g in range(2):
                        ins = mm(PU[1][:, T * g:T * g + T], PW[:, 2 * h + g, :], P_X[:, 2 * h + g, :])
                    ins.then_inc(S("pool_mm"), 1)

            def attn1_scores(h):
                o, i = 64 * (h % 2), h // 2
                s = PU[0]
                if h == 0:
                    pe.wait_ge(S("stage_copied"), 4)
                    pe.wait_ge(S("sel_ready"), 1)
                else:
                    pe.wait_ge(S("p_exp"), h)
                kw = dict(start=False, stop=True, skip_group_check=True)
                mm(s[:, 0:P], QT1[o:o + 64, i, 0:P], KT1[o:o + 64, i, 0:P])
                mm(s[:, P:3 * P], QT1[o:o + 64, i, P:T], KT1[o:o + 64, i, :], **kw)
                mm(s[:, 0:P], ident[:, :], CM[:, :], **kw)
                mm(s[:, 2 * P:3 * P], ident[:, :], CM[:, :], **kw)
                mm(s[:, 0:P], SEL[:, h, :], CUMT[:, 0:P], **kw)
                mm(s[:, P:3 * P], SEL[:, h, :], CUMT[:, :], **kw)\
                    .then_inc(S("scored"), 1)

            def attn1():
                for h in range(8):
                    q0 = HQ1 + 5 * h
                    if h == 0:
                        yield q0
                        attn1_scores(0)
                    yield q0 + 4
                    pe.wait_ge(S("p_ready"), h + 1)
                    if h:
                        pe.wait_ge(S("pT_ready"), h)
                    for i in range(3):
                        ins = tr(PT[0][:, P * i:P * i + P], PB[h % 2][:, P * i:P * i + P])
                    ins.then_inc(S("p_transposed"), 1)
                    if h + 1 < 8:
                        yield q0 + 5
                        attn1_scores(h + 1)
                    yield q0 + 6
                    pe.wait_ge(S("pT_ready"), h + 1)
                    pe.wait_ge(evict["act"], find[(1, "v", 0)].evicted)
                    i, o = h // 2, 64 * (h % 2)
                    if i >= 1:
                        pe.wait_ge(yready(1, 3), i)
                    y = PT[1][o:o + 64, T * (i % 2):T * (i % 2) + T]
                    mm(y, V1[:, 0, 64 * h:64 * h + 64], PTB[h % 2][:, 0:T])
                    mm(y[:, P:T], V1[:, 1, 64 * h:64 * h + 64], PTB[h % 2][:, T:3 * P], start=False,
                       skip_group_check=True)\
                        .then_inc(S("attn_mm"), 1)

            def s5():
                for n in range(10):
                    yield BQ[n]
                    src, i = MT_SRC[n]
                    if n:
                        pe.wait_ge(S("s5_mT_copied"), n)
                    pe.wait_ge(S("c_pad"), 1)
                    if n >= 4:
                        pe.wait_ge(S("b_pad"), 1)
                    if n >= 8:
                        pe.wait_ge(S("gm_w_tril"), 1)
                    for f in range(4):
                        ins = tr(PT[1][:, P * f:P * f + P], src[:, CH * i + P * f:CH * i + P * f + P])
                    ins.then_inc(S("s5_mT"), 1)

            def s5_in():
                for j in range(32):
                    yield S5Q + 2 * j
                    i, c = j // 4, 32 * (j % 4)
                    if j == 0:
                        pe.wait_ge(S("s5_mT_copied"), 8)
                        pe.wait_ge(S("stage_copied"), sbase[2] + 4)
                    if j >= 2:
                        pe.wait_ge(S("s5_bu_read"), j - 1)
                    for r in range(2):
                        ins = mm(PU[j % 2][:, T * r:T * r + T], BT[r][c:c + 32, i, :], XI[c:c + 32, i, :],
                                 tile_position=(c, 0))
                    ins.then_inc(S("bu_mm"), 1)

            def s5_out():
                for j in range(32):
                    yield S5Q + 2 * j + 7
                    i, c = j // 4, 32 * (j % 4)
                    pe.wait_ge(S("s5_state_ready"), j + 1)
                    if j == 0:
                        pe.wait_ge(S("s5_mT_copied"), 10)
                    if j % 4 == 0 and i:
                        pe.wait_ge(S("s5_y"), i)
                    if st["sb"]:
                        pe.wait_ge(yready(2, 2), st["sb"])
                    for r in range(2):
                        ins = mm(PT[1][c:c + 32, 0:T], CT[r][:, i, c:c + 32], STATE[:, r, :], start=r == 0, stop=r == 1,
                                 tile_position=(0, c))
                    ins.then_inc(S("s5_read"), 1)
                    st["s5_out"] = j + 1

            def attn2():
                z = PT[0]
                for h in range(8):
                    q0 = HQ2 + 6 * h
                    yield q0
                    if h == 0:
                        pe.wait_ge(S("stage_copied"), sbase[2] + 12)
                        pe.wait_ge(S("masks_ready"), 1)
                    else:
                        pe.wait_ge(S("sb_w"), h)
                    mm(z[:, 0:T], KT2[:, h, 0:P], QT2[:, h, :])
                    mm(z[:, T:3 * P], KT2[:, h, P:T], QT2[:, h, P:T], start=False, skip_group_check=True)\
                        .then_inc(S("z_mm"), 1)
                    yield q0 + 3
                    pe.wait_ge(S("sp_ready"), h + 1)
                    kw = dict(start=False, stop=True, skip_group_check=True)
                    mm(z[:, 0:T], NLOW[:, :], A_E[:, 0:T], **kw)
                    mm(z[:, P:T], NONE[:, :], A_E[:, T:3 * P], **kw)
                    mm(z[:, T:3 * P], NLOW[:, :], A_E[:, T:3 * P], **kw)
                    mm(z[:, 0:P], ident[:, :], SM[:, :], **kw)
                    mm(z[:, T:3 * P], ident[:, :], SM[:, :], **kw).then_inc(S("tri_mm"), 1)
                    yield q0 + 6
                    pe.wait_ge(S("sb_w"), h + 1)
                    pe.wait_ge(evict["act"], find[(2, "v", h // 4)].evicted)
                    if h:
                        pe.wait_ge(yready(2, 2), h)
                    if st["s5_out"] >= 4:
                        pe.wait_ge(S("s5_y"), st["s5_out"] // 4)
                    y = PT[1][:, T:2 * T]
                    mm(y, VT[:, 0, P * h:P * h + P], A_W[:, 0:T])
                    mm(y[:, P:T], VT[:, 1, P * h:P * h + P], A_W[:, T:3 * P], start=False,
                       skip_group_check=True).then_inc(S("sb_mm"), 1)
                    st["sb"] = h + 1

            def gmlp():
                for n in range(4):
                    yield GQ + 2 * n
                    t, g0 = n // 2, 4 * (n % 2)
                    pe.wait_ge(S("gm_normed"), 2)
                    if n >= 2:
                        pe.wait_ge(S("gm_y"), n - 1)
                    for g in range(4):
                        ins = mm(PU[n % 2][:, P * g:P * g + P], GW[:, g0 + g, :], GV[:, t, P * (g0 + g):P * (g0 + g) + P])
                    ins.then_inc(S("gm_mixed"), 1)
                for n in range(4):
                    yield GQ + 8 + 2 * n
                    pe.wait_ge(S("gm_y"), 4)
                    if n >= 2:
                        pe.wait_ge(yready(2, 0), n - 1)
                    for k in range(UK):
                        for t in range(NT):
                            ins = tr(PU[n % 2][:, T * k + P * t:T * k + P * t + P],
                                     GU[:, t, P * (2 * n + k):P * (2 * n + k) + P])
                    ins.then_inc(S("gm_T"), 1)

            def glu_out():
                for i in range(4):
                    yield n_a[2] + GLUQ[i]
                    pe.wait_ge(evict["act"], find[(2, "glu", i // 2)].evicted)
                    if i >= 2:
                        pe.wait_ge(S("glu_sig"), i - 1)
                    else:
                        pe.wait_ge(yready(2, 2), 8)
                    for k in range(UK):
                        for t in range(NT):
                            ins = tr(PT[i % 2][:, T * k + P * t:T * k + P * t + P],
                                     ST[i // 2][:, t, P * (2 * (i % 2) + k):P * (2 * (i % 2) + k) + P])
                    ins.then_inc(S("glu_T"), 1)

            def merge(b, before):
                for i, q in enumerate(merge_positions(b)):
                    yield q
                    pe.wait_ge(S("tmp_added"), before + (gates_of(b) - 1) * (i // 2 + 1))
                    if i == 0 and b == 2:
                        pe.wait_ge(S("glu_sig"), 4)
                    g = ts0[b] + 8 + i
                    pe.wait_ge(ts_split, g - 1)
                    pair(g, i % 2, M, 2 * P * i)
                pe.wait_ge(ts_split, ts0[b] + 16)

            def mlp(b):
                H0, e0 = ts0[b] + 24, down0[b]
                H1, H2 = YH, YL

                def split(j, r):
                    pe.wait_ge(ts_split, j * 2 + (H0 + r - 1))
                    pair(None, r, HB[1], 2 * P * r)

                def down(j, base, i0):
                    pe.wait_ge(ts_split, j * 2 + (H0 + 2))
                    for i in range(8):
                        n = i // 2
                        if i % 2 == 0:
                            pe.wait_ge(evict["dve"], j * 4 + (e0 + n - 1))
                        unit(base, i0 + i, H1, H2, UK * (i % 2), PA[n % 2], i % 2 == 0, i % 2 == 1)

                def body(j):
                    base = mlp_base(b, j)
                    pe.wait_ge(S(f"relu{b}_ready"), j + 1)
                    for i in range(4):
                        unit(base, i, XH, XL, UK * i, PU, i == 0, False)
                    pe.wait_ge(S(f"hidden{b}_ready"), j + 1)
                    split(j, 0)
                    split(j, 1)
                    for i in range(4, 8):
                        unit(base, i, XH, XL, UK * i, PU, False, i == 7)
                    down(j, base, 8)

                for i in range(8):
                    unit(0, u0[b, "m"] + i, XH, XL, UK * i, PU, i == 0, i == 7)
                with pe.Fori(0, NF - 1) as j:
                    body(j)
                pe.wait_ge(S(f"hidden{b}_ready"), NF)
                split(NF - 1, 0)
                split(NF - 1, 1)
                down(NF - 1, mlp_base(b, NF - 1), 0)

            pe.wait_ge(S("masks_ready"), 1)
            pe.wait_ge(S("dt_rows"), 1)
            tr(PT[0][:, 0:P], slot(Z, 0)[:, 0:P])
            nc.tensor.transpose(PT[0][:, P:P + 96], slot(Z, 0)[0:96, P:2 * P], ident[0:96, 0:96]).then_inc(S("vectors_mm"), 1)
            pe.wait_ge(S("vA_ready"), 1)
            before = 0
            for b in blocks:
                norm(ts0[b])
                gens = [Steps(g) for g in ([stage_transposes(b)] + (
                    [lru(), attn1()] if b == 1 else [s5(), s5_in(), s5_out(), attn2(), gmlp(), glu_out()])
                    + [merge(b, before)])]
                before += NCH * (gates_of(b) - 1)
                waited = False
                for ch in plan[b, "a"] + plan[b, "b"]:
                    if ch.n >= 2 and chunks[ch.n - 2] is not None:
                        pe.wait_ge(evict[chunks[ch.n - 2].by], chunks[ch.n - 2].evicted)
                    if ch.tag[0] == "prod":
                        pe.wait_ge(yready(b, ch.tag[2]), YN[b, ch.tag[2]])
                    if ch.tag[0] == "glu":
                        pe.wait_ge(S("s5_g_split"), 1)
                    lh, ll = (XH, XL) if ch.lhs == "X" else (YH, YL)
                    for i in range(ch.nu):
                        unit(0, ch.u0 + i, lh, ll, ch.l0 + UK * i, PA[ch.n % 2], i == 0, i == ch.nu - 1)
                        for g in gens:
                            g.upto(ch.u0 + i - u0[b, "a"])
                norm(ts0[b] + 16)
                mlp(b)


_INS = ["x", "norm_mix_g", "w_in", "lru_conv_w", "lru_conv_b", "lru_wr", "lru_br", "lru_wi", "lru_bi", "lru_lambda",
        "pool_w", "pool_scale", "sconv_w", "q_norm_g", "k_norm_g", "forget_b", "w_branch", "w_out", "norm_mlp_g",
        "w_mlp_up", "w_mlp_down", "norm1_g_2", "w_in_2", "b_gate_2", "gm_norm_g_2", "gm_w_s_2", "gm_b_s_2",
        "s5_lambda_re_2", "s5_lambda_im_2", "s5_log_dt_2", "s5_b_re_2", "s5_b_im_2", "s5_c_re_2", "s5_c_im_2",
        "s5_d_2", "s5_w_glu_2", "s5_b_glu_2", "w_branch_2", "w_out_2", "norm2_g_2", "w_mlp_in_2", "w_mlp_out_2",
        "final_g_2"]


def kernel(**inputs):
    import numpy as _np
    import concourse.bacc as _bacc
    from concourse import mybir as _mybir
    from concourse.bass_utils import run_bass_kernel_spmd as _run

    nc = _bacc.Bacc("TRN2", target_bir_lowering=False, num_devices=1)
    arrays, aps = {}, {}
    for name in _INS:
        a = _np.ascontiguousarray(inputs[name])
        arrays[f"in_{name}"] = a
        aps[name] = nc.dram_tensor(f"in_{name}", a.shape, _mybir.dt.from_np(a.dtype), kind="ExternalInput").ap()
    aps["x1"] = nc.dram_tensor("x1", (T, D), _mybir.dt.float32, kind="Internal").ap()
    out = nc.dram_tensor("out_0", (1, T, D), _mybir.dt.float32, kind="ExternalOutput").ap()
    build(nc, aps, out)
    r = _run(nc, [arrays], core_ids=[0])
    return r.results[0]["out_0"]
```

```python
import concourse.bass as bass
from concourse import mybir
from contextlib import ExitStack

F32 = mybir.dt.float32
F32R = mybir.dt.float32r
ACT = mybir.ActivationFunctionType
ALU = mybir.AluOpType
AX = mybir.AxisListType.X

P = 128
T = 256
NT = T // P
D = 2048
KD = D // P
CH = 512
UK = 2
NCH = D // CH
FF = 8192
NF = FF // CH
RING = 4
EPS = 1e-6
SL = 1024
NEG = -1.0e30


class Steps:

    def __init__(self, gen):
        self.gen = gen
        self.at = next(gen, None)

    def upto(self, p):
        while self.at is not None and self.at <= p:
            self.at = next(self.gen, None)


def build(nc, A, out):
    with ExitStack() as ctx:
        def sb(name, shape, dt=F32):
            return ctx.enter_context(nc.sbuf_tensor(name, shape, dt))

        sems = {}

        def S(name):
            if name not in sems:
                sems[name] = ctx.enter_context(nc.semaphore(name))
            return sems[name]

        raw = sb("raw", [P, RING, UK * CH])
        whi = sb("whi", [P, RING, UK * CH], F32R)
        wlo = sb("wlo", [P, RING, UK * CH], F32R)
        XH = sb("XH", [P, KD, T], F32R)
        XL = sb("XL", [P, KD, T], F32R)
        NY = 24
        with nc.sbuf_tensor("Z", [P, 2 * NY * T], F32) as Z:
            pass
        Y = sb("Y", [P, 2 * NY * T], F32R)
        YH = Y[:, 0:NY * T].rearrange("p (k t) -> p k t", t=T)
        YL = Y[:, NY * T:2 * NY * T].rearrange("p (k t) -> p k t", t=T)
        G = sb("G", [P, 4 * SL])
        NA = 14
        W = sb("W", [P, NA * SL])
        ident = sb("ident", [P, P])
        UP = sb("UP", [P, T])
        NLOW = sb("NLOW", [P, P])
        CM = sb("CM", [P, P])
        SM = sb("SM", [P, P])
        S01 = sb("S01", [P, P])
        NONE = sb("NONE", [P, P])
        small = sb("small", [P, 400])
        qg = sb("qg", [P, 2, 64])
        wf = sb("wf", [P, KD, 8])
        wfh = sb("wfh", [P, KD, 8], F32R)
        wfl = sb("wfl", [P, KD, 8], F32R)

        banks = ctx.enter_context(nc.psum_tensor("banks", [P, 8, CH], F32))
        PA = [[banks[:, 2 * b + t, :] for t in range(NT)] for b in range(2)]
        PU = [banks[:, 4 + t, :] for t in range(NT)]
        PT = [banks[:, 6 + t, :] for t in range(NT)]

        off = [0]

        def vec(n):
            off[0] += n
            return small[:, off[0] - n:off[0]]

        ss, rs = vec(2), vec(2)
        vA, vB = vec(P), vec(96)
        conv_w, conv_b, br, bi, lam = vA[:, 0:16], vA[:, 16:20], vA[:, 20:24], vA[:, 24:28], vA[:, 28:32]
        pscale, sconv_w = vA[:, 32:36], vA[:, 36:48]
        s5_d, b_glu, gm_b, even = vA[:, 48:56], vA[:, 56:64], vA[:, 64:72], vA[:, 96:97]
        lam_re, lam_im, log_dt = vB[:, 0:32], vB[:, 32:64], vB[:, 64:96]
        s16, r16 = vec(16), vec(16)
        mx, rsm = vec(2), vec(2)
        fb = vec(8)
        mag = vec(32)
        odd = vec(1)
        nbr = vec(8)
        sq = vec(NT * NCH)

        def slot(t, i, n=1):
            return t[:, SL * i:SL * (i + n)]

        def ft(ap):
            return ap.rearrange("p (f t) -> p f t", t=T)

        def tok(ap, c=CH):
            return ap.rearrange("p (t c) -> p t c", c=c)

        X = tok(slot(W, 0, 4), D)
        XN = tok(slot(W, 4, 4), D)
        GB = slot(W, 8, 2)
        HB = [tok(slot(W, 4 + i)) for i in range(2)]
        M = tok(slot(W, 6, 4), D)
        TMP = [tok(slot(W, 10 + i)) for i in range(2)]
        ST = [tok(slot(W, i)) for i in range(2)]
        GT = [tok(slot(G, k)) for k in range(4)]

        def rows(name):
            return A[name][0].rearrange("(k p) n -> p k n", p=P)

        class Chunk:
            def __init__(self, w, col, nu, lhs, l0, by, tag):
                self.w, self.col, self.nu, self.lhs, self.l0, self.by, self.tag = w, col, nu, lhs, l0, by, tag

        w_in, w_in2 = rows("w_in"), rows("w_in_2")
        wo, wo2 = rows("w_out"), rows("w_out_2")
        wb = [A["w_branch"][0, k].rearrange("(k p) n -> p k n", p=P) for k in range(4)]
        wb2 = [A["w_branch_2"][0, k].rearrange("(k p) n -> p k n", p=P) for k in range(3)]
        wglu = rows("s5_w_glu_2")
        proj1 = [Chunk(w_in, c, 8, "X", 0, "act", (tag, 0)) for tag, c in (
            ("q", 2560), ("k", 3072), ("v", 3584), ("xa", 0), ("xp", 512), ("gc", 1536), ("xc", 2048), ("gb", 1024))]
        FCOL, GATE1, GATE2 = 4096, 4104, 6144

        def gates1(n):
            return [Chunk(w_in, GATE1 + D * k + CH * n, 8, "X", 0, "act", ("gate", n, k)) for k in range(4)]

        def prods1(n):
            return [Chunk(wb[k], CH * n, 2, "Y", 4 * k, "dve", ("prod", n, k)) for k in range(4)]

        proj2 = [Chunk(w_in2, base + CH * h, 8, "X", 0, "act", (tag, h)) for tag, base in (
            ("s5", 2048), ("q", 3072), ("k", 4096), ("v", 5120), ("gv", 1024), ("u", 0)) for h in range(2)]

        def gates2(n):
            return [Chunk(w_in2, GATE2 + D * k + CH * n, 8, "X", 0, "dve", ("gate", n, k)) for k in range(3)]

        def prods2(n):
            return [Chunk(wb2[k], CH * n, 4, "Y", 8 * k, "dve", ("prod", n, k)) for k in (2, 0, 1)]

        glu = [Chunk(wglu, CH * h, 4, "Y", 8, "act", ("glu", h)) for h in range(2)]

        def outs(w):
            return [Chunk(w, CH * n, 8, "X", 0, "dve", ("out", n)) for n in range(NCH)]

        plan = {(1, "a"): proj1 + gates1(0),
                (1, "b"): prods1(0) + sum((gates1(n) + prods1(n) for n in range(1, NCH)), []) + outs(wo),
                (2, "a"): proj2 + gates2(0),
                (2, "b"): glu + prods2(0) + sum((gates2(n) + prods2(n) for n in range(1, NCH)), []) + outs(wo2)}
        blocks = (1, 2)
        u0, ts0, down0, find = {}, {}, {}, {}
        u = ts = 0
        counts = {"act": 0, "dve": 0}
        chunks = []
        for b in blocks:
            for ph in "ab":
                u0[b, ph] = u
                for ch in plan[b, ph]:
                    counts[ch.by] += 1
                    ch.n, ch.u0, ch.evicted = len(chunks), u, counts[ch.by]
                    chunks.append(ch)
                    find[(b,) + ch.tag] = ch
                    u += ch.nu
            u0[b, "m"] = u
            u += NF * 16
            down0[b] = counts["dve"]
            counts["dve"] += NF * NCH
            chunks += [None] * (len(chunks) % 2)
            ts0[b] = ts
            ts += 24 + 2 * NF
        evict = {"act": S("acc_read_by_act"), "dve": S("acc_read_by_dve")}
        raw_in = [S(f"raw_in{i}") for i in range(RING)]
        hi_done, lo_done, used = S("whi_ready"), S("wlo_ready"), S("units_multiplied")
        ts_ready, ts_split = S("transposed"), S("transposes_split")
        NB = len(blocks)
        XS = [A["x"][0], A["x1"]]

        def gates_of(b):
            return 4 if b == 1 else 3

        def mlp_base(b, j):
            return j * 16 + (u0[b, "m"] + 8)

        def yready(b, k):
            return S(f"y{b}{k}_ready")

        QT1, KT1 = ft(slot(Z, 4)), ft(slot(Z, 5))
        PB = [slot(Z, 10)[:, 384 * i:384 * i + 384] for i in range(2)]
        PTB = [slot(Z, 11)[:, 384 * i:384 * i + 384] for i in range(2)]
        CUMT = slot(Z, 10)[0:8, 768:1024]
        LZ, LE, LH, LQ, LS = (slot(Z, 11)[:, 768 + 20 * i:788 + 20 * i] for i in range(5))
        Q1, K1, V1 = (tok(slot(W, i)) for i in (11, 12, 13))
        L_X, L_U, L_R, L_G, L_T, L_A = (ft(slot(W, i)) for i in (2, 3, 4, 5, 6, 7))
        P_X, P_P, P_Q = (ft(slot(W, i)) for i in (8, 9, 10))
        S_C, S_Y, S_B = (ft(slot(W, i)) for i in (11, 12, 2))
        BD = slot(G, 0).rearrange("p (w f c) -> p w f c", w=2, f=4)
        PW = slot(G, 1)[:, 0:512].rearrange("p (g j) -> p g j", g=4)
        SEL = slot(G, 2)[0:8, :].rearrange("p (h c) -> p h c", h=8)
        CNT = slot(G, 3)[:, 0:16]
        LRUQ, PMQ, HQ1 = [48, 57, 66, 75], [78, 81], 30
        XI, GS, SG = ft(slot(W, 2, 2)), ft(slot(W, 4, 2)), ft(slot(W, 2, 2))
        QT2, KT2 = ft(slot(W, 9, 2)), ft(slot(W, 11, 2))
        A_E, A_W = slot(W, 13)[:, 0:384], slot(W, 13)[:, 384:768]
        VT, GV, GU = tok(slot(Z, 0, 2), 1024), tok(slot(Z, 6, 2), 1024), tok(slot(W, 0, 2), 1024)
        GMG = slot(W, 6)
        BT = [slot(Z, 2 + r).rearrange("p (i c) -> p i c", i=8) for r in range(2)]
        CT = [slot(Z, 8 + r).rearrange("p (i c) -> p i c", i=8) for r in range(2)]
        GW = slot(G, 3).rearrange("p (g c) -> p g c", g=8)
        BPAD = [slot(W, 4 + r) for r in range(2)]
        CPAD = [slot(W, 9 + r) for r in range(2)]
        BSRC = slot(Z, 10).rearrange("p (r j h) -> p r j h", r=2, j=32)
        CSRC = slot(Z, 4).rearrange("p (r i q) -> p r i q", r=2, i=8)
        GWSRC = slot(Z, 6).rearrange("p (g s) -> p g s", g=8)
        PLO = slot(Z, 11)[:, 0:256].rearrange("p (r k j) -> p r k j", r=2, k=4)
        PHI = slot(W, 13)[:, 768:1024].rearrange("p (r k j) -> p r k j", r=2, k=4)
        D_S, D_C, D_N = (slot(Z, 5)[:, 288 * i:288 * i + 288] for i in range(3))
        D_DT, D_X, D_TH, D_R, D_I = (slot(Z, 5)[:, 864 + 32 * i:896 + 32 * i] for i in range(5))
        D_KR, D_KI, D_D, D_U, D_V = (slot(Z, 11)[:, 256 + 32 * i:288 + 32 * i] for i in range(5))
        BTMP = slot(Z, 11)[:, 512:1024]
        NTAB, TG = 5, 8
        TAB = [G[:, 512 * i:512 * i + 512].rearrange("p (r t) -> p r t", r=2) for i in range(NTAB)]
        TNEW = [slot(G, 2 * r, 2).rearrange("p (j t) -> p j t", t=T) for r in range(2)]
        ROT = [slot(W, 7)[:, 512 * i:512 * i + 512].rearrange("p (r t) -> p r t", r=2) for i in range(2)]
        D1, D2 = (slot(W, 6)[:, 512 * i:512 * i + 512].rearrange("p (r t) -> p r t", r=2) for i in range(2))
        STATE = [m.rearrange("p (r t) -> p r t", r=2) for m in (slot(W, 8)[:, 0:512], slot(G, 2)[:, 512:1024])]
        STMP = slot(W, 8)[:, 512:1024].rearrange("p (r t) -> p r t", r=2)
        PARQ = 104
        S5Q, HQ2, GQ = 26, 57, 104
        S5_TILES = 32
        GLUQ = [8, 9, 11, 12]
        n_a = {b: u0[b, "b"] - u0[b, "a"] for b in blocks}
        BQ = [6 + 2 * n for n in range(10)]
        MT_SRC = [(m, i) for m in (CPAD[0], CPAD[1], BPAD[0], BPAD[1], slot(Z, 6)) for i in range(2)]
        MT_DST = [slot(m, j)[:, CH * i:CH * i + CH] for m, j in ((Z, 8), (Z, 9), (Z, 2), (Z, 3), (G, 3)) for i in range(2)]
        TP = {1: [(tag, t, q + 3 * t) for tag, q in (("q", 14), ("k", 22), ("xa", 34), ("xp", 42), ("gc", 51),
                                                     ("xc", 60), ("gb", 69)) for t in range(NT)],
              2: [((tag, h), t, 8 * c + 10 + 3 * t) for c, (tag, h) in enumerate(
                  (tg, hh) for tg in ("s5", "q", "k") for hh in range(2)) for t in range(NT)]}
        TDST = {1: {"q": QT1, "k": KT1, "xa": L_X, "xp": P_X, "gc": S_C, "xc": S_Y, "gb": S_B},
                2: {(tg, h): m[:, 4 * h:4 * h + 4, :] for tg, m in (("s5", XI), ("q", QT2), ("k", KT2)) for h in range(2)}}
        TBANK = {1: PU[1], 2: PT[0]}
        sbase = {1: 0, 2: len(TP[1]) if len(blocks) > 1 else 0}
        stage_base = {1: 4, 2: sbase[2]}
        YN = {(1, 0): 1, (1, 1): 1, (1, 2): 1, (1, 3): 4, (2, 0): 4, (2, 1): 4, (2, 2): 8}

        def bias_buf(n, k):
            if n == 0:
                return slot(W, 7, 2)[:, CH * k:CH * k + CH]
            return slot(W, 12)[:, CH * ((3 * n + k) % 2):CH * ((3 * n + k) % 2) + CH]

        def end_of(b, ch):
            return ch.u0 + ch.nu - u0[b, "a"]

        def merge_positions(b):
            p3 = find[(b, "prod", NCH - 1, 0 if b == 1 else 2)].u0 - u0[b, "a"]
            po = find[(b, "out", 0)].u0 - u0[b, "a"]
            return [p3 + 1 + i for i in range(6)] + [po + 3] * 2

        block = ctx.enter_context(nc.Block())

        @block.sync
        def _(sp_):
            def load(base, i, view):
                if not (isinstance(base, int) and base + i < RING):
                    sp_.wait_ge(lo_done, base + (i - RING + 1))
                sp_.dma_start(raw[:, i % RING, :].rearrange("p (k n) -> p k n", n=CH), view)\
                   .then_inc(raw_in[i % RING], 16)

            def tables():
                for j in range(S5_TILES):
                    yield S5Q + 2 * j + 1 if j >= NTAB else 6 + j
                    if j == 0:
                        sp_.wait_ge(S("tables_saved"), 32 * S5_TILES // TG)
                    if j >= NTAB:
                        sp_.wait_ge(S("s5_state_ready"), j - NTAB + 1)
                    sp_.dma_start(TAB[j % NTAB], A["tables"][j]).then_inc(S(f"table_in{j % NTAB}"), 16)

            for n in range(NCH):
                sp_.dma_start(X[:, :, CH * n:CH * n + CH],
                              A["x"][0, :, CH * n:CH * n + CH].rearrange("(t p) n -> p t n", p=P)).then_inc(S(f"first_x{n}_in"), 16)
            for b in blocks:
                branch = Steps(tables() if b == 2 else iter(()))
                for ph in "ab":
                    for ch in plan[b, ph]:
                        for i in range(ch.nu):
                            load(0, ch.u0 + i, ch.w[:, UK * i:UK * i + UK, ch.col:ch.col + CH])
                            branch.upto(ch.u0 + i - u0[b, "a"])
                up = rows("w_mlp_up" if b == 1 else "w_mlp_in_2")
                dn = rows("w_mlp_down" if b == 1 else "w_mlp_out_2")
                for i in range(8):
                    load(0, u0[b, "m"] + i, up[:, UK * i:UK * i + UK, 0:CH])
                with sp_.Fori(0, NF - 1) as j:
                    for i in range(8):
                        load(mlp_base(b, j), i, up[:, UK * i:UK * i + UK, bass.ds(j * CH + CH, CH)])
                    for i in range(8):
                        n = i // 2
                        load(mlp_base(b, j), 8 + i, dn[:, bass.ds(j * 4 + UK * (i % 2), UK), CH * n:CH * n + CH])
                for i in range(8):
                    n, k = i // 2, 4 * (NF - 1) + UK * (i % 2)
                    load(mlp_base(b, NF - 1), i, dn[:, k:k + UK, CH * n:CH * n + CH])
            for n in range(NCH):
                sp_.wait_ge(S("normed"), NCH * 2 * NB + n + 1)
                sp_.dma_start(out[0, :, CH * n:CH * n + CH].rearrange("(t p) n -> p t n", p=P),
                              XN[:, :, CH * n:CH * n + CH]).then_inc(S("out_written"), 16)
            sp_.wait_ge(S("out_written"), 16 * NCH)

        @block.gpsimd
        def _(pool):
            count = [0]

            def chain(ins):
                count[0] += 1
                ins.then_inc(S("pool_chain"), 1)
                pool.wait_ge(S("pool_chain"), count[0])

            tt = nc.gpsimd.tensor_tensor
            gains = [A["norm_mix_g"][0], A["norm_mlp_g"][0], A["norm1_g_2"][0], A["norm2_g_2"][0]]
            gains = ({1: gains[:2], 2: gains[2:]}[blocks[0]] if NB == 1 else gains) + [A["final_g_2"]]

            def load_gain(m):
                pool.dma_start(GB, gains[m].partition_broadcast(P)).then_inc(S("gain_in"), 16)

            for m, v in ((ident, 0.0), (UP, 1.0), (NLOW, -1.0), (CM, 0.0), (SM, 0.0), (S01, 1.0)):
                chain(nc.gpsimd.memset(m[:, :], v))
            for m, op, fill, base, step, cm in (
                    (ident, ALU.not_equal, 1.0, 0, -1, 1), (UP, ALU.is_ge, 0.0, 0, 1, -1),
                    (NLOW, ALU.is_ge, 0.0, 0, -1, 1), (CM, ALU.is_ge, NEG, 0, -1, 1),
                    (SM, ALU.is_gt, NEG, 0, 1, -1), (S01, ALU.is_gt, 0.0, 0, 1, -1)):
                chain(nc.gpsimd.affine_select(out=m[:, :], in_=m[:, :], compare_op=op, fill=fill, base=base,
                                              pattern=[[step, m.shape[1]]], channel_multiplier=cm))
            nc.gpsimd.memset(NONE[:, :], -1.0).then_inc(S("masks_ready"), 1)
            va, vb = slot(Z, 0)[:, 0:P], slot(Z, 0)[:, P:2 * P]
            ld = slot(Z, 0)[:, 2 * P:2 * P + 2]
            chain(nc.gpsimd.memset(va, 0.0))
            chain(nc.gpsimd.memset(va[96:128, :].rearrange("p (a b c) -> p a b c", b=2, c=16)[:, :, 0, :], 1.0))
            at = 0
            for name in ("lru_conv_w", "lru_conv_b", "lru_br", "lru_bi", "lru_lambda", "pool_scale", "sconv_w",
                         "s5_d_2", "s5_b_glu_2", "gm_b_s_2"):
                src = A[name][0]
                src = src.rearrange("(f p) -> f p", p=P) if len(src.shape) == 1 else \
                    src.rearrange("k (f p) -> (k f) p", p=P)
                n = src.shape[0]
                pool.dma_start(va[at:at + n, :], src).then_inc(S("vectors_in"), 16)
                at += n
            pool.dma_start(vb[0:32, :], A["s5_lambda_re_2"][0].rearrange("(j g) p -> j (g p)", g=2)).then_inc(S("vectors_in"), 16)
            pool.dma_start(vb[32:64, :], A["s5_lambda_im_2"][0].rearrange("(j g) p -> j (g p)", g=2)).then_inc(S("vectors_in"), 16)
            pool.dma_start(ld[64:96, :], A["s5_log_dt_2"][0].rearrange("(j g) -> j g", g=2)).then_inc(S("vectors_in"), 16)

            def block1():
                bd = BD
                chain(nc.gpsimd.memset(slot(G, 0), 0.0))
                for w, name in enumerate(("lru_wr", "lru_wi")):
                    for half in range(2):
                        pool.dma_start(bd[64 * half:64 * half + 64, w, :, 64 * half:64 * half + 64],
                                       A[name][0].rearrange("(f a) i j -> a i f j", a=2)[half]).then_inc(S("small1_in"), 16)
                pool.dma_start(slot(G, 1)[:, 0:512].rearrange("p (g j) -> p g j", g=4),
                               A["pool_w"][0].rearrange("g i j -> i g j")).then_inc(S("small1_in"), 16)
                sel = slot(G, 2)[0:8, :].rearrange("p (h c) -> p h c", h=8)
                chain(nc.gpsimd.memset(sel, 0.0))
                chain(nc.gpsimd.affine_select(out=sel, in_=sel, compare_op=ALU.not_equal, fill=-1.0, base=0,
                                              pattern=[[-1, 8], [0, P]], channel_multiplier=1))
                nc.gpsimd.iota(slot(G, 3)[:, 0:16], [[1, 16]], base=1, channel_multiplier=0,
                               allow_small_or_imprecise_dtypes=True).then_inc(S("sel_ready"), 1)

            def block2():
                pool.wait_ge(S("vA_ready"), 1)
                pool.wait_ge(used, u0[2, "a"])
                bsrc = BSRC
                for r, name in enumerate(("s5_b_re_2", "s5_b_im_2")):
                    pool.dma_start(bsrc[:, r], A[name][0].rearrange("(j g) p h -> (g p) j h", g=2)).then_inc(S("small2_in"), 16)
                csrc = CSRC
                for r, name in enumerate(("s5_c_re_2", "s5_c_im_2")):
                    pool.dma_start(csrc[:, r], A[name][0].rearrange("(i g) h q -> (g h) i q", i=8)).then_inc(S("small2_in"), 16)
                gw = GWSRC
                pool.dma_start(gw, A["gm_w_s_2"][0].rearrange("g t s -> t g s")).then_inc(S("small2_in"), 16)
                pool.wait_ge(S("small2_in"), 16 * 5)
                nc.gpsimd.affine_select(out=gw, in_=gw, compare_op=ALU.is_ge, fill=0.0, base=0,
                                        pattern=[[0, 8], [-1, P]], channel_multiplier=1).then_inc(S("gm_w_tril"), 1)
                for j in range(S5_TILES):
                    tab, r, state = TAB[j % NTAB], ROT[j % 2], STATE[j % 2]
                    c, s = (tab[:, i].unsqueeze(1).to_broadcast([P, 2, T]) for i in range(2))
                    pool.wait_ge(S("s5_r_ready"), j + 1)
                    if j >= 2:
                        pool.wait_ge(S("s5_read"), j - 1)
                    tt(state, r, c, ALU.mult)
                    chain(tt(STMP, r, s, ALU.mult))
                    tt(state[:, 0], state[:, 0], STMP[:, 1], ALU.subtract)
                    tt(state[:, 1], state[:, 1], STMP[:, 0], ALU.add).then_inc(S("s5_state_ready"), 1)
                    pool.wait_ge(S("s5_state_ready"), j + 1)
                pool.wait_ge(S("s5_read"), 32)
                pool.dma_start(GMG, A["gm_norm_g_2"][0].partition_broadcast(P)).then_inc(S("gm_gain_in"), 16)
                for k in range(3):
                    load_bias(0, k)

            def make_tables():
                ta, tb = slot(W, 10), slot(W, 11)
                pool.wait_ge(S("powers_ready"), 1)
                for g in range(S5_TILES // TG):
                    c, s = TNEW
                    if g:
                        pool.wait_ge(S("tables_saved"), 32 * g)
                    nc.gpsimd.memset(c[:, :, 0:1], 1.0)
                    chain(nc.gpsimd.memset(s[:, :, 0:1], 0.0))
                    for k in range(8):
                        n, pw = 1 << k, (PLO if k < 4 else PHI)[:, :, k % 4, TG * g:TG * g + TG]
                        a_ = ta[:, 0:TG * n].rearrange("p (j l) -> p j l", j=TG)
                        b_ = tb[:, 0:TG * n].rearrange("p (j l) -> p j l", j=TG)
                        pc, ps = (pw[:, i].unsqueeze(2).to_broadcast([P, TG, n]) for i in range(2))
                        c0, s0 = c[:, :, 0:n], s[:, :, 0:n]
                        tt(a_, c0, pc, ALU.mult)
                        chain(tt(b_, s0, ps, ALU.mult))
                        chain(tt(c[:, :, n:2 * n], a_, b_, ALU.subtract))
                        tt(a_, c0, ps, ALU.mult)
                        chain(tt(b_, s0, pc, ALU.mult))
                        chain(tt(s[:, :, n:2 * n], a_, b_, ALU.add))
                    for i, m in enumerate(TNEW):
                        pool.dma_start(A["tables"][TG * g:TG * g + TG, :, i, :].rearrange("j p t -> p j t"), m)\
                            .then_inc(S("tables_saved"), 16)
                pool.wait_ge(S("tables_saved"), 32 * S5_TILES // TG)

            def load_bias(n, k):
                pool.dma_start(bias_buf(n, k), A["b_gate_2"][0, k, CH * n:CH * n + CH].partition_broadcast(P))\
                    .then_inc(S(f"bias_in{k}"), 16)

            def load_biases(lo, hi):
                for i in range(lo, hi):
                    if i >= 5:
                        g = find[(2, "gate", (i - 2) // 3, (i - 2) % 3)]
                        pool.wait_ge(evict["dve"], g.evicted)
                    load_bias(i // 3, i % 3)

            added = 0
            for bi_, b in enumerate(blocks):
                (block1 if b == 1 else block2)()
                for k in range(gates_of(b)):
                    pool.wait_ge(yready(b, k), YN[b, k])
                if b == 2:
                    load_biases(3, 5)
                pool.dma_start(X, XS[bi_ if NB > 1 else 0].rearrange("(t p) n -> p t n", p=P)).then_inc(S("x_in"), 16)
                for n in range(NCH):
                    order = [0, 1, 2, 3] if b == 1 else [2, 0, 1]
                    m = M[:, :, CH * n:CH * n + CH]
                    for k in order[1:]:
                        added += 1
                        pool.wait_ge(evict["dve"], find[(b, "prod", n, k)].evicted)
                        tt(m, m, TMP[added % 2], ALU.add).then_inc(S("tmp_added"), 1)
                        pool.wait_ge(S("tmp_added"), added)
                    if b == 2 and n + 1 < NCH:
                        load_biases(3 * n + 5, min(3 * n + 8, 12))
                pool.wait_ge(ts_split, ts0[b] + 16)
                load_gain(2 * bi_ + 1)
                pool.wait_ge(S("normed"), NCH * (2 * bi_ + 2))
                load_gain(2 * bi_ + 2)
                if b != blocks[-1]:
                    make_tables()
                    pool.wait_ge(evict["dve"], down0[b] + NF * NCH)
                    pool.dma_start(A["x1"].rearrange("(t p) n -> p t n", p=P), X).then_inc(S("x_saved"), 16)
                    pool.wait_ge(S("x_saved"), 16)

        @block.scalar
        def _(act):
            st = {"hi": 0, "sq": 0, "norm": 0, "n": 0}

            def chain(ins):
                st["n"] += 1
                ins.then_inc(S("act_chain"), 1)
                act.wait_ge(S("act_chain"), st["n"])

            def a(out_, in_, f=ACT.Copy, **kw):
                return nc.scalar.activation(out_, in_, f, **kw)

            def hi(base, i):
                act.wait_ge(raw_in[i % RING], base * 4 + (16 * (i // RING) + 16))
                if not (isinstance(base, int) and base + i < RING):
                    act.wait_ge(used, base + (i - RING + 1))
                a(whi[:, i % RING, :], raw[:, i % RING, :]).then_inc(hi_done, 1)

            def hi_upto(n):
                while st["hi"] < n:
                    hi(0, st["hi"])
                    st["hi"] += 1

            def squares(n, need):
                act.wait_ge(*need)
                if st["sq"]:
                    act.wait_ge(S("squares"), st["sq"])
                for t in range(NT):
                    a(slot(W, 12)[:, CH * t:CH * t + CH], X[:, t, CH * n:CH * n + CH], ACT.Square,
                      accum_out=sq[:, NCH * t + n:NCH * t + n + 1]).then_inc(S("squares"), 1)
                st["sq"] += NT

            def root():
                st["norm"] += 1
                act.wait_ge(S("mean_square"), st["norm"])
                a(rs, rs, ACT.Sqrt).then_inc(S("root"), 1)

            def out_squares(b):
                for n in range(NCH - 1):
                    ch = find[(b, "out", n)]
                    yield end_of(b, ch) + 4
                    squares(n, (evict["dve"], ch.evicted))

            def staged(ch, dst, f=ACT.Copy, **kw):
                act.wait_ge(used, ch.u0 + ch.nu)
                for t in range(NT):
                    ins = a(dst[:, t, :], PA[ch.n % 2][t], f, **kw)
                ins.then_inc(evict["act"], 1)

            def evictions(b):
                stages = 0
                for ch in plan[b, "a"] + plan[b, "b"]:
                    tag, h = ch.tag[0], ch.tag[1]
                    if tag == "gate" and b == 2:
                        yield end_of(b, ch) + 4
                        act.wait_ge(evict["dve"], ch.evicted)
                        a(GT[ch.tag[2]], GT[ch.tag[2]], ACT.Sigmoid).then_inc(S("gates_ready2"), 1)
                        continue
                    if ch.by != "act":
                        continue
                    yield end_of(b, ch) + 3
                    if tag == "gate":
                        n, k = ch.tag[1:]
                        if n == 0:
                            act.wait_ge(S(("lru_mm", "pool_mm", "scored", "pool_done")[k]), (4, 2, 8, 1)[k])
                            staged(ch, GT[k])
                            if k == 3:
                                for kk in range(4):
                                    act.wait_ge(evict["act"], ch.evicted)
                                    a(GT[kk], GT[kk], ACT.Sigmoid).then_inc(S("gates_ready1"), 1)
                        else:
                            act.wait_ge(evict["dve"], find[(1, "prod", n - 1, k)].evicted)
                            staged(ch, GT[k], ACT.Sigmoid)
                    elif b == 1 and tag in "qkv":
                        staged(ch, {"q": Q1, "k": K1, "v": V1}[tag])
                    elif tag == "v":
                        staged(ch, VT[:, :, CH * h:CH * h + CH])
                    elif tag == "gv":
                        if h == 0:
                            act.wait_ge(S("s5_mT"), 10)
                        staged(ch, GV[:, :, CH * h:CH * h + CH], ACT.Gelu_apprx_tanh)
                    elif tag == "u":
                        if h == 0:
                            act.wait_ge(S("stage_transposed"), sbase[2] + len(TP[2]))
                        staged(ch, GU[:, :, CH * h:CH * h + CH], ACT.Gelu_apprx_tanh)
                    elif tag == "glu":
                        act.wait_ge(S("gm_T"), 4)
                        staged(ch, ST[h])
                    else:
                        if b != blocks[0] and stages == 0:
                            act.wait_ge(S("x_saved"), 16)
                        if stages >= 2:
                            act.wait_ge(S("stage_transposed"), stage_base[b] + 2 * (stages - 1))
                        staged(ch, ST[stages % 2])
                        stages += 1

            def copies(b):
                for n, (tag, t, q) in enumerate(TP[b]):
                    yield q + 2
                    act.wait_ge(S("stage_transposed"), sbase[b] + n + 1)
                    if tag == "gb":
                        act.wait_ge(S("lru_u"), 1)
                    scale = 128.0 ** -0.5 if tag[0] == "q" and b == 2 else 1.0
                    a(TDST[b][tag][:, :, P * t:P * t + P], TBANK[b].rearrange("p (f t) -> p f t", t=P),
                      scale=scale).then_inc(S("stage_copied"), 1)

            def lru():
                yield 1
                act.wait_ge(S("wf_in"), 16)
                a(wfh[:, :, :], wf[:, :, :]).then_inc(S("wf_hi"), 1)
                yield 8
                act.wait_ge(S("f_mm"), 1)
                a(CUMT, PU[1][0:8, 0:T]).then_inc(S("f_copied"), 1)
                yield 11
                act.wait_ge(S("z_ready"), 1)
                chain(a(LE, LZ, ACT.Abs))
                a(LE, LE, ACT.Exp, scale=-1.0).then_inc(S("z_exp"), 1)
                yield 15
                act.wait_ge(S("cum_mm"), 1)
                a(CUMT, PU[1][0:8, 0:T]).then_inc(S("cumT_ready"), 1)
                for f in range(4):
                    yield LRUQ[f] + 2
                    act.wait_ge(S("lru_mm"), f + 1)
                    a(L_R[:, f, :], PU[1][:, 0:T], ACT.Exp, scale=-1.0, bias=nbr[:, f:f + 1])
                    a(L_G[:, f, :], PU[1][:, T:2 * T], ACT.Exp, scale=-1.0, bias=nbr[:, 4 + f:5 + f]).then_inc(S("lru_exp"), 1)
                yield LRUQ[3] + 3
                act.wait_ge(S("log_a"), 1)
                a(L_T, L_R, ACT.Tanh).then_inc(S("lru_tanh"), 1)
                a(L_A, L_R, ACT.Exp).then_inc(S("lru_a"), 1)
                yield LRUQ[3] + 6
                act.wait_ge(S("lru_1ma2"), 1)
                a(L_R, L_T, ACT.Sqrt).then_inc(S("lru_sqrt"), 1)
                yield LRUQ[3] + 12
                act.wait_ge(S("lru_h"), 1)
                a(YH[:, 0:4, :], L_U).then_inc(S("y_hi10"), 1)

            def pool_sconv():
                for h in range(2):
                    yield PMQ[h] + 2
                    act.wait_ge(S("pool_mm"), h + 1)
                    for g in range(2):
                        ins = a(P_P[:, 2 * h + g, :], PU[1][:, T * g:T * g + T], scale=pscale[:, 2 * h + g:2 * h + g + 1])
                    ins.then_inc(S("pool_scaled"), 1)
                act.wait_ge(S("pool_scaled"), 2)
                a(YH[:, 4:8, :], P_P).then_inc(S("y_hi11"), 1)
                yield 83
                act.wait_ge(S("sconv_ready"), 1)
                a(YH[:, 8:12, :], S_Y).then_inc(S("y_hi12"), 1)

            def attn1():
                yield 12
                for i in range(2):
                    yield 12 + 8 * i
                    act.wait_ge(S("qk_ms"), i + 1)
                    a(r16, s16, ACT.Sqrt).then_inc(S("qk_root"), 1)
                for h in range(8):
                    q0 = HQ1 + 5 * h
                    yield q0 + 2
                    act.wait_ge(S("row_max"), h + 1)
                    p_ = PB[h % 2]
                    if h >= 2:
                        act.wait_ge(S("p_transposed"), h - 1)
                    a(p_[:, 0:P], PU[0][:, 0:P], ACT.Exp, bias=mx[:, 0:1], accum_out=rsm[:, 0:1])
                    a(p_[:, P:3 * P], PU[0][:, P:3 * P], ACT.Exp, bias=mx[:, 1:2], accum_out=rsm[:, 1:2]).then_inc(S("p_exp"), 1)
                    yield q0 + 5
                    act.wait_ge(S("p_transposed"), h + 1)
                    if h >= 2:
                        act.wait_ge(S("attn_mm"), h - 1)
                    a(PTB[h % 2], PT[0][:, 0:3 * P]).then_inc(S("pT_ready"), 1)
                    if h % 2:
                        yield q0 + 8
                        act.wait_ge(S("attn_mm"), h + 1)
                        i = h // 2
                        a(YH[:, 12 + i, :], PT[1][:, T * (i % 2):T * (i % 2) + T]).then_inc(S("y_hi13"), 1)

            def s5_params():
                yield PARQ
                act.wait_ge(S("attn_mm"), 8)
                a(D_DT, log_dt, ACT.Exp).then_inc(S("s5_dt"), 1)
                act.wait_ge(S("s5_x"), 1)
                a(D_TH, D_X, ACT.Tanh, scale=0.5)
                a(mag, D_X, ACT.Exp).then_inc(S("s5_mag"), 1)
                yield PARQ + 2
                act.wait_ge(S("s5_reduced"), 1)
                a(D_C, D_S, ACT.Abs).then_inc(S("s5_abs"), 1)
                act.wait_ge(S("s5_cos_arg"), 1)
                a(D_C, D_C, ACT.Sin)
                a(D_S, D_S, ACT.Sin).then_inc(S("s5_sin"), 1)

            def s5a():
                for n in range(10):
                    yield BQ[n] + 2
                    act.wait_ge(S("s5_mT"), n + 1)
                    a(MT_DST[n], PT[1]).then_inc(S("s5_mT_copied"), 1)
                yield S5Q + 74
                act.wait_ge(S("s5_y"), 8)
                a(GS, GS, ACT.Gelu_apprx_tanh).then_inc(S("s5_g"), 1)
                act.wait_ge(S("s5_g"), 1)
                a(YH[:, 8:16, :], GS).then_inc(S("s5_g_hi"), 1)

            def attn2():
                for h in range(8):
                    q0 = HQ2 + 6 * h
                    yield q0 + 2
                    act.wait_ge(S("z_mm"), h + 1)
                    if h:
                        act.wait_ge(S("tri_mm"), h)
                    chain(a(A_E, PT[0][:, 0:384], ACT.Abs))
                    chain(a(A_E, A_E, ACT.Exp, scale=-1.0))
                    a(A_E, A_E, ACT.Ln, bias=1.0).then_inc(S("ln_ready"), 1)
                    yield q0 + 5
                    act.wait_ge(S("tri_mm"), h + 1)
                    if h:
                        act.wait_ge(S("sb_mm"), h)
                    a(A_W, PT[0][:, 0:384], ACT.Exp).then_inc(S("sb_w"), 1)
                    yield q0 + 8
                    act.wait_ge(S("sb_mm"), h + 1)
                    a(YH[:, 16 + h, :], PT[1][:, T:2 * T]).then_inc(S("y_hi22"), 1)

            def gmlp():
                yield GQ - 5
                act.wait_ge(S("s5_bu_read"), 32)
                act.wait_ge(evict["act"], find[(2, "gv", 1)].evicted)
                for t in range(NT):
                    a(banks[:, 4:6, :], GV[:, t, :].rearrange("p (a c) -> p a c", a=2), ACT.Square,
                      accum_out=ss[:, t:t + 1]).then_inc(S("gm_squares"), 1)
                    act.wait_ge(S("gm_squares"), t + 1)
                yield GQ - 2
                act.wait_ge(S("gm_ms"), 1)
                a(rs, rs, ACT.Sqrt).then_inc(S("gm_root"), 1)
                for n in range(4):
                    yield GQ + 10 + 2 * n
                    act.wait_ge(S("gm_T"), n + 1)
                    if n == 0:
                        act.wait_ge(S("sb_mm"), 8)
                    a(YH[:, 2 * n:2 * n + 2, :], PU[n % 2].rearrange("p (k t) -> p k t", t=T)).then_inc(S("y_hi20"), 1)

            def glu_out():
                for i in range(4):
                    yield n_a[2] + GLUQ[i] + 2
                    act.wait_ge(S("glu_T"), i + 1)
                    for kk in range(2):
                        f = 2 * i + kk
                        ins = a(SG[:, f, :], PT[i % 2][:, T * kk:T * kk + T], ACT.Sigmoid, bias=b_glu[:, f:f + 1])
                    ins.then_inc(S("glu_sig"), 1)
                    yield n_a[2] + GLUQ[i] + 3
                    act.wait_ge(S("glu_y"), i + 1)
                    a(YH[:, 8 + 2 * i:10 + 2 * i, :], GS[:, 2 * i:2 * i + 2, :]).then_inc(S("y_hi21"), 1)

            def merge_hi(b):
                for i, q in enumerate(merge_positions(b)):
                    yield q + (2 if i < 6 else 1)
                    split_hi(ts0[b] + 8 + i, XH[:, UK * i:UK * i + UK, :])

            def split_hi(q, dst):
                act.wait_ge(ts_ready, q + 1)
                a(dst, PT[q % 2].rearrange("p (k t) -> p k t", t=T)).then_inc(S("ts_hi"), 1)

            def mlp(b):
                H0 = ts0[b] + 24

                def split_pair(j, r):
                    act.wait_ge(ts_ready, j * 2 + (H0 + r + 1))
                    a(YH[:, UK * r:UK * r + UK, :], PT[r].rearrange("p (k t) -> p k t", t=T)).then_inc(S("ts_hi"), 1)

                def relu(base, n):
                    act.wait_ge(used, base + 8)
                    for t in range(NT):
                        ins = a(HB[0][:, t, :], PU[t], ACT.Relu)
                    ins.then_inc(S(f"relu{b}_ready"), 1)

                def body(j):
                    base = mlp_base(b, j)
                    for i in range(7):
                        hi(base, i)
                    split_pair(j, 0)
                    split_pair(j, 1)
                    for i in range(7, 12):
                        hi(base, i)
                    relu(base, j + 1)
                    for i in range(12, 16):
                        hi(base, i)

                hi_upto(u0[b, "m"] + 8)
                for i in range(4):
                    hi(mlp_base(b, 0), i)
                relu(u0[b, "m"], 0)
                base = mlp_base(b, 0)
                for i in range(4, 7):
                    hi(base, i)
                split_pair(0, 0)
                split_pair(0, 1)
                for i in range(7, 12):
                    hi(base, i)
                relu(base, 1)
                for i in range(12, 16):
                    hi(base, i)
                with act.Fori(1, NF - 1) as j:
                    body(j)
                base = mlp_base(b, NF - 1)
                for i in range(4):
                    hi(base, i)
                split_pair(NF - 1, 0)
                split_pair(NF - 1, 1)
                for i in range(4, 8):
                    hi(base, i)
                st["hi"] = base + 8
                for n in range(NCH):
                    squares(n, (evict["dve"], down0[b] + 4 * (NF - 1) + n + 1))
                    if b != blocks[-1] and 1 <= n < 3:
                        hi_upto(base + 8 + (1, 3)[n - 1])

            act.dma_start(GB, A["norm_mix_g"][0].partition_broadcast(P)).then_inc(S("first_gain_in"), 16)
            act.dma_start(wf[:, :, :], w_in[:, :, FCOL:FCOL + 8]).then_inc(S("wf_in"), 16)
            act.dma_start(fb, A["forget_b"][0].partition_broadcast(P)).then_inc(S("head_gains_in"), 16)
            for i, name in enumerate(("q_norm_g", "k_norm_g")):
                act.dma_start(qg[:, i, :], A[name][0].partition_broadcast(P)).then_inc(S("head_gains_in"), 16)
            for bi_, b in enumerate(blocks):
                if bi_ == 0:
                    for n in range(NCH):
                        squares(n, (S(f"first_x{n}_in"), 16))
                root()
                hi_upto(u0[b, "a"] + RING)
                for i in range(8):
                    split_hi(ts0[b] + i, XH[:, UK * i:UK * i + UK, :])
                gens = [Steps(g) for g in ([evictions(b), copies(b)] + (
                    [attn1(), lru(), pool_sconv(), s5_params()] if b == 1 else [s5a(), attn2(), gmlp(), glu_out()]) + [merge_hi(b), out_squares(b)])]
                for p_ in range(u0[b, "m"] - u0[b, "a"]):
                    hi_upto(u0[b, "a"] + p_ + 1)
                    for g in gens:
                        g.upto(p_)
                for g in gens:
                    g.upto(10 ** 6)
                hi_upto(u0[b, "m"] + RING - 1)
                squares(NCH - 1, (evict["dve"], find[(b, "out", NCH - 1)].evicted))
                root()
                hi_upto(u0[b, "m"] + RING)
                for i in range(8):
                    split_hi(ts0[b] + 16 + i, XH[:, UK * i:UK * i + UK, :])
                mlp(b)
            root()

        @block.vector
        def _(dve):
            st = {"lo": 0, "norm": 0, "n": 0, "added": 0}
            tt, ts, stt = nc.vector.tensor_tensor, nc.vector.tensor_scalar, nc.vector.scalar_tensor_tensor

            def chain(ins):
                st["n"] += 1
                ins.then_inc(S("dve_chain"), 1)
                dve.wait_ge(S("dve_chain"), st["n"])

            def lo(base, i):
                dve.wait_ge(hi_done, base + (i + 1))
                tt(wlo[:, i % RING, :], raw[:, i % RING, :], whi[:, i % RING, :].bitcast(F32), ALU.subtract)\
                    .then_inc(lo_done, 1)

            def lo_upto(n):
                while st["lo"] < n:
                    lo(0, st["lo"])
                    st["lo"] += 1

            def split_lo(q, r, hi_, dst):
                dve.wait_ge(S("ts_hi"), q + 1)
                tt(dst, PT[r].rearrange("p (k t) -> p k t", t=T), hi_.bitcast(F32), ALU.subtract).then_inc(ts_split, 1)

            def norm():
                m = st["norm"]
                st["norm"] += 1
                dve.wait_ge(S("squares"), NT * NCH * (m + 1))
                chain(nc.vector.tensor_reduce(ss, sq.rearrange("p (t n) -> p t n", t=NT), AX, ALU.add))
                ts(rs, ss, 1.0 / D, EPS, ALU.mult, ALU.add).then_inc(S("mean_square"), 1)
                dve.wait_ge(S("root"), m + 1)
                chain(nc.vector.reciprocal(rs, rs))
                dve.wait_ge(S("gain_in") if m else S("first_gain_in"), 16 * max(m, 1))
                for n in range(NCH):
                    cols = slice(CH * n, CH * n + CH)
                    for t in range(NT):
                        ins = stt(XN[:, t, cols], X[:, t, cols], rs[:, t:t + 1], GB[:, cols], ALU.mult, ALU.mult)
                    ins.then_inc(S("normed"), 1)

            def evictions(b):
                order = [0, 1, 2, 3] if b == 1 else [2, 0, 1]
                for ch in plan[b, "a"] + plan[b, "b"]:
                    if ch.by != "dve":
                        continue
                    acc = PA[ch.n % 2]
                    if ch.tag[0] == "gate":
                        yield end_of(b, ch) + 3
                        n, k = ch.tag[1:]
                        dve.wait_ge(used, ch.u0 + ch.nu)
                        dve.wait_ge(S(f"bias_in{k}"), 16 * (n + 1))
                        if n == 0:
                            dve.wait_ge(S("s5_state_ready"), 32)
                        for t in range(NT):
                            ins = tt(GT[k][:, t, :], acc[t], bias_buf(n, k), ALU.add)
                    elif ch.tag[0] == "prod":
                        yield end_of(b, ch) + 2
                        n, k = ch.tag[1:]
                        dve.wait_ge(used, ch.u0 + ch.nu)
                        if b == 1 and n > 0:
                            dve.wait_ge(evict["act"], find[(1, "gate", n, k)].evicted)
                        else:
                            dve.wait_ge(S(f"gates_ready{b}"), (4 if b == 1 else 3) * n + k + 1)
                        if k == order[0]:
                            dst = M[:, :, CH * n:CH * n + CH]
                        else:
                            st["added"] += 1
                            dst = TMP[st["added"] % 2]
                            if st["added"] > 2:
                                dve.wait_ge(S("tmp_added"), st["added"] - 2)
                        for t in range(NT):
                            ins = tt(dst[:, t, :], acc[t], GT[k][:, t, :], ALU.mult)
                    else:
                        yield end_of(b, ch) + 3
                        n = ch.tag[1]
                        dve.wait_ge(used, ch.u0 + ch.nu)
                        dve.wait_ge(S("x_in"), 16 * (blocks.index(b) + 1))
                        for t in range(NT):
                            x = X[:, t, CH * n:CH * n + CH]
                            ins = tt(x, acc[t], x, ALU.add)
                    ins.then_inc(evict["dve"], 1)

            def merge_lo(b):
                for i, q in enumerate(merge_positions(b)):
                    yield q + (2 if i < 6 else 1)
                    split_lo(ts0[b] + 8 + i, i % 2, XH[:, UK * i:UK * i + UK, :], XL[:, UK * i:UK * i + UK, :])

            def y_lo(b, k, kt, n, src, hi_count):
                dve.wait_ge(S(f"y_hi{b}{k}"), hi_count)
                tt(YL[:, kt:kt + n, :], src, YH[:, kt:kt + n, :].bitcast(F32), ALU.subtract).then_inc(yready(b, k), 1)

            def vectors():
                yield 2
                dve.wait_ge(S("vectors_in"), 16 * 13)
                vb3 = slot(Z, 0)[64:96, P:2 * P].rearrange("p (g e) -> p g e", g=2)
                nc.vector.tensor_copy(vb3, slot(Z, 0)[64:96, 2 * P:2 * P + 2].unsqueeze(2).to_broadcast([32, 2, 64]))\
                    .then_inc(S("dt_rows"), 1)
                yield 5
                dve.wait_ge(S("vectors_mm"), 1)
                chain(nc.vector.tensor_copy(vA, PT[0][:, 0:P]))
                nc.vector.tensor_copy(vB, PT[0][:, P:P + 96])
                ts(odd, even, -1.0, 1.0, ALU.mult, ALU.add).then_inc(S("vA_ready"), 1)

            def lru():
                yield 6
                dve.wait_ge(S("wf_hi"), 1)
                tt(wfl[:, :, :], wf[:, :, :], wfh[:, :, :].bitcast(F32), ALU.subtract).then_inc(S("wf_split"), 1)
                yield 11
                dve.wait_ge(S("head_gains_in"), 16 * 3)
                dve.wait_ge(S("f_transposed"), 1)
                dve.wait_ge(S("vA_ready"), 1)
                tt(LZ[:, 0:16].rearrange("p (t h) -> p t h", t=2), PU[1][:, 0:16].rearrange("p (t h) -> p t h", t=2),
                   fb.unsqueeze(1).to_broadcast([P, 2, 8]), ALU.add)
                ts(nbr, vA[:, 20:28], -1.0, None, ALU.mult)
                nc.vector.tensor_copy(LZ[:, 16:20], lam).then_inc(S("z_ready"), 1)
                yield 12
                dve.wait_ge(S("z_exp"), 1)
                chain(ts(LH, LE, 2.0, None, ALU.add))
                chain(nc.vector.reciprocal(LH, LH))
                chain(tt(LE, LE, LH, ALU.mult))
                chain(tt(LQ, LE, LE, ALU.mult))
                chain(ts(LH, LQ, 2.0 / 17, None, ALU.mult))
                for c in (15, 13, 11, 9, 7, 5, 3):
                    chain(stt(LH, LH, 2.0 / c, LQ, ALU.add, ALU.mult))
                chain(stt(LH, LH, 2.0, LE, ALU.add, ALU.mult))
                chain(stt(LS, LZ, 0.0, LH, ALU.min, ALU.subtract))
                ts(LS[:, 16:20], LS[:, 16:20], 8.0, None, ALU.mult).then_inc(S("log_f"), 1)
                for f in range(4):
                    yield 40 + f
                    dve.wait_ge(S("stage_copied"), 6)
                    x, u_ = L_X[:, f, :], L_U[:, f, :]
                    chain(ts(u_, x, conv_w[:, 12 + f:13 + f], conv_b[:, f:f + 1], ALU.mult, ALU.add))
                    for k in (2, 1, 0):
                        s = 3 - k
                        ins = stt(u_[:, s:T], x[:, 0:T - s], conv_w[:, 4 * k + f:4 * k + f + 1], u_[:, s:T], ALU.mult, ALU.add)
                        if k or f < 3:
                            chain(ins)
                ins.then_inc(S("lru_u"), 1)
                for f in range(4):
                    r_, g_ = L_R[:, f, :], L_G[:, f, :]
                    yield LRUQ[f] + 3
                    dve.wait_ge(S("lru_exp"), f + 1)
                    ts(g_, g_, 1.0, None, ALU.add)
                    chain(ts(r_, r_, 1.0, None, ALU.add))
                    nc.vector.reciprocal(g_, g_)
                    chain(nc.vector.reciprocal(r_, r_))
                    ins = ts(r_, r_, LS[:, 16 + f:17 + f], None, ALU.mult)
                    if f == 3:
                        ins.then_inc(S("log_a"), 1)
                    chain(tt(g_, g_, L_U[:, f, :], ALU.mult))
                yield LRUQ[3] + 5
                dve.wait_ge(S("lru_a"), 1)
                chain(tt(L_U, L_A, L_A, ALU.mult))
                chain(stt(L_T, L_U, 1.0, L_T, ALU.add, ALU.mult))
                ts(L_T, L_T, -1.0, 1.3e-35, ALU.mult, ALU.max).then_inc(S("lru_1ma2"), 1)
                yield LRUQ[3] + 7
                dve.wait_ge(S("lru_sqrt"), 1)
                chain(tt(L_G, L_G, L_R, ALU.mult))
                for f in range(4):
                    yield LRUQ[3] + 8 + f
                    ins = nc.vector.tensor_tensor_scan(L_U[:, f, :], L_A[:, f, :], L_G[:, f, :], 0.0, ALU.mult, ALU.add)
                ins.then_inc(S("lru_h"), 1)
                yield LRUQ[3] + 13
                y_lo(1, 0, 0, 4, L_U, 1)

            def pool():
                yield 48
                dve.wait_ge(S("sel_ready"), 1)
                chain(nc.vector.reciprocal(CNT, CNT))
                dve.wait_ge(S("stage_copied"), 8)
                src, dst = P_X, P_P
                for i, s in enumerate((1, 2, 4, 8)):
                    yield 49 + i
                    nc.vector.tensor_copy(dst[:, i:4, 0:s], src[:, i:4, 0:s])
                    chain(tt(dst[:, i:4, s:T], src[:, i:4, s:T], src[:, i:4, 0:T - s], ALU.add))
                    src, dst = dst, (P_Q if dst is P_P else P_P)
                for g in range(4):
                    yield 53 + g
                    win = 2 << g
                    w_ = (P_P if g % 2 == 0 else P_Q)[:, g, :]
                    chain(tt(w_[:, 0:win - 1], w_[:, 0:win - 1], CNT[:, 0:win - 1], ALU.mult))
                    x = P_X[:, g, :]
                    tt(x[:, 0:win - 1], w_[:, 0:win - 1], x[:, 0:win - 1], ALU.subtract)
                    ins = stt(x[:, win - 1:T], w_[:, win - 1:T], 1.0 / win, x[:, win - 1:T], ALU.mult, ALU.subtract)
                ins.then_inc(S("pool_done"), 1)
                yield PMQ[1] + 4
                y_lo(1, 1, 4, 4, P_P, 1)

            def sconv():
                yield 66
                dve.wait_ge(S("stage_copied"), 12)
                chain(tt(S_C, S_C, S_Y, ALU.mult))
                for f in range(4):
                    yield 67 + f
                    x, y = S_C[:, f, :], S_Y[:, f, :]
                    chain(ts(y, x, sconv_w[:, 8 + f:9 + f], None, ALU.mult))
                    for k in (1, 0):
                        s = 2 - k
                        chain(stt(y[:, s:T], x[:, 0:T - s], sconv_w[:, 4 * k + f:4 * k + f + 1], y[:, s:T], ALU.mult, ALU.add))
                yield 75
                dve.wait_ge(S("stage_copied"), 14)
                tt(S_Y, S_Y, S_B, ALU.mult).then_inc(S("sconv_ready"), 1)
                yield 85
                y_lo(1, 2, 8, 4, S_Y, 1)

            def attn1():
                for i, (m, f) in enumerate(((Q1, 1.0 / 8), (K1, 1.0))):
                    yield 12 + 8 * i
                    c = plan[1, "a"][i]
                    dve.wait_ge(evict["act"], c.evicted)
                    flat = slot(W, 11 + i).rearrange("p (g e) -> p g e", e=64)
                    sq = slot(W, 3)
                    chain(tt(sq, slot(W, 11 + i), slot(W, 11 + i), ALU.mult))
                    chain(nc.vector.tensor_reduce(s16, sq.rearrange("p (g e) -> p g e", e=64), AX, ALU.add))
                    ts(s16, s16, 1.0 / 64, EPS, ALU.mult, ALU.add).then_inc(S("qk_ms"), 1)
                    dve.wait_ge(S("qk_root"), i + 1)
                    chain(nc.vector.reciprocal(r16, r16))
                    if i == 0:
                        chain(ts(r16, r16, f, None, ALU.mult))
                    yield 13 + 8 * i
                    chain(tt(flat, flat, r16.unsqueeze(2).to_broadcast([P, 16, 64]), ALU.mult))
                    tt(flat, flat, qg[:, i, :].unsqueeze(1).to_broadcast([P, 16, 64]), ALU.mult).then_inc(S("qk_normed"), 1)
                for h in range(8):
                    q0 = HQ1 + 5 * h
                    yield q0 + 2
                    dve.wait_ge(S("scored"), h + 1)
                    if h:
                        dve.wait_ge(S("p_exp"), h)
                    nc.vector.tensor_reduce(mx[:, 0:1], PU[0][:, 0:P], AX, ALU.max)
                    chain(nc.vector.tensor_reduce(mx[:, 1:2], PU[0][:, P:3 * P], AX, ALU.max))
                    ts(mx, mx, -1.0, None, ALU.mult).then_inc(S("row_max"), 1)
                    yield q0 + 3
                    dve.wait_ge(S("p_exp"), h + 1)
                    p_ = PB[h % 2]
                    chain(nc.vector.reciprocal(rsm, rsm))
                    ts(p_[:, 0:P], p_[:, 0:P], rsm[:, 0:1], None, ALU.mult)
                    ts(p_[:, P:3 * P], p_[:, P:3 * P], rsm[:, 1:2], None, ALU.mult).then_inc(S("p_ready"), 1)
                    if h % 2:
                        yield q0 + 8
                        i = h // 2
                        y_lo(1, 3, 12 + i, 1, PT[1][:, T * (i % 2):T * (i % 2) + T].unsqueeze(1), i + 1)

            def s5_params():
                yield PARQ
                dve.wait_ge(S("s5_dt"), 1)
                tt(D_X, lam_re, D_DT, ALU.mult).then_inc(S("s5_x"), 1)
                chain(tt(D_C[:, 32:64], lam_im, D_DT, ALU.mult))
                for k in range(8):
                    ts(D_S[:, 32 * k + 32:32 * k + 64], D_C[:, 32:64], float(1 << k), None, ALU.mult)
                chain(ts(D_S[:, 0:32], D_C[:, 32:64], 0.5, None, ALU.mult))
                magic = 1.5 * 2.0 ** 23
                chain(ts(D_N, D_S, 0.15915494309189535, magic, ALU.mult, ALU.add))
                chain(ts(D_N, D_N, magic, None, ALU.subtract))
                for c in (6.28125, 1.934051513671875e-3, 1.2556658656e-06):
                    chain(stt(D_S, D_N, -c, D_S, ALU.mult, ALU.add))
                ts(D_S, D_S, 3.1415925, -3.1415925, ALU.min, ALU.max).then_inc(S("s5_reduced"), 1)
                yield PARQ + 2
                dve.wait_ge(S("s5_abs"), 1)
                ts(D_C, D_C, -1.0, 1.5707963705062866, ALU.mult, ALU.add).then_inc(S("s5_cos_arg"), 1)
                yield PARQ + 4
                dve.wait_ge(S("s5_sin"), 1)
                for r, m in enumerate((D_C, D_S)):
                    nc.vector.tensor_copy(PLO[:, r], m[:, 32:160].rearrange("p (k j) -> p k j", k=4))
                    ins = nc.vector.tensor_copy(PHI[:, r], m[:, 160:288].rearrange("p (k j) -> p k j", k=4))
                ins.then_inc(S("powers_ready"), 1)
                dve.wait_ge(S("s5_mag"), 1)
                cs, sn, sh = D_C[:, 32:64], D_S[:, 32:64], D_S[:, 0:32]
                chain(stt(D_R, mag, 1.0, D_TH, ALU.add, ALU.mult))
                chain(tt(D_R, D_R, cs, ALU.mult))
                chain(tt(D_U, sh, sh, ALU.mult))
                chain(stt(D_R, D_U, -2.0, D_R, ALU.mult, ALU.add))
                tt(D_I, mag, sn, ALU.mult)
                tt(D_U, lam_re, lam_re, ALU.mult)
                chain(tt(D_V, lam_im, lam_im, ALU.mult))
                chain(tt(D_D, D_U, D_V, ALU.add))
                chain(nc.vector.reciprocal(D_D, D_D))
                for dst, p, q, op in ((D_KR, D_R, D_I, ALU.add), (D_KI, D_I, D_R, ALU.subtract)):
                    tt(D_U, p, lam_re, ALU.mult)
                    chain(tt(D_V, q, lam_im, ALU.mult))
                    chain(tt(D_U, D_U, D_V, op))
                    chain(tt(dst, D_U, D_D, ALU.mult))

            def s5():
                yield 1
                dve.wait_ge(S("small2_in"), 16 * 5)
                for r in range(2):
                    sgn = 1.0 if r == 0 else -1.0
                    for q in range(2):
                        v = CPAD[r].rearrange("p (i q e) -> p i q e", i=8, q=2)[:, :, q, :]
                        ins = ts(v, CSRC[:, r], (even, odd)[q], sgn, ALU.mult, ALU.mult)
                ins.then_inc(S("c_pad"), 1)
                yield 5
                def mul(dst, kk, r):
                    return tt(dst, BSRC[:, r], kk.unsqueeze(2).to_broadcast([P, 32, 16]), ALU.mult)
                b3 = BTMP.rearrange("p (j h) -> p j h", j=32)
                acc3 = slot(W, 6)[:, 0:512].rearrange("p (j h) -> p j h", j=32)
                for r in range(2):
                    chain(nc.vector.memset(BPAD[r], 0.0))
                    chain(mul(acc3, D_KR, r))
                    chain(mul(b3, D_KI, 1 - r))
                    chain(tt(acc3, acc3, b3, ALU.subtract if r == 0 else ALU.add))
                    pad = BPAD[r].rearrange("p (j q h) -> p j q h", j=32, q=2)
                    for q in range(2):
                        ins = nc.vector.tensor_copy(pad[64 * q:64 * q + 64, :, q, :], acc3[64 * q:64 * q + 64])
                    if r:
                        ins.then_inc(S("b_pad"), 1)
                    else:
                        chain(ins)
                for j in range(32):
                    if j >= 7 and j % 4 == 3:
                        yield S5Q + 2 * j + 1
                        skip(j // 4 - 1)
                    yield S5Q + 2 * j + 2
                    c, s = (TAB[j % NTAB][:, i].unsqueeze(1).to_broadcast([P, 2, T]) for i in range(2))
                    bu = PU[j % 2].rearrange("p (r t) -> p r t", r=2)
                    dve.wait_ge(S("bu_mm"), j + 1)
                    dve.wait_ge(S(f"table_in{j % NTAB}"), 16 * (j // NTAB + 1))
                    tt(D1, bu, c, ALU.mult)
                    tt(D2, bu, s, ALU.mult).then_inc(S("s5_bu_read"), 1)
                    dve.wait_ge(S("s5_bu_read"), j + 1)
                    tt(D1[:, 0], D1[:, 0], D2[:, 1], ALU.add)
                    chain(tt(D1[:, 1], D1[:, 1], D2[:, 0], ALU.subtract))
                    if j >= 2:
                        dve.wait_ge(S("s5_state_ready"), j - 1)
                    m = mag[:, j:j + 1].to_broadcast([P, T])
                    nc.vector.tensor_tensor_scan(ROT[j % 2][:, 0], m, D1[:, 0], 0.0, ALU.mult, ALU.add)
                    nc.vector.tensor_tensor_scan(ROT[j % 2][:, 1], m, D1[:, 1], 0.0, ALU.mult, ALU.add).then_inc(S("s5_r_ready"), 1)
                    dve.wait_ge(S("s5_r_ready"), j + 1)
                yield S5Q + 72
                skip(7)

            def skip(i):
                dve.wait_ge(S("s5_read"), 4 * i + 4)
                stt(GS[:, i, :], XI[:, i, :], s5_d[:, i:i + 1], PT[1][:, 0:T], ALU.mult, ALU.add).then_inc(S("s5_y"), 1)

            def attn2():
                for h in range(8):
                    q0 = HQ2 + 6 * h
                    yield q0 + 2
                    dve.wait_ge(S("ln_ready"), h + 1)
                    chain(stt(A_E, PT[0][:, 0:384], 0.0, A_E, ALU.max, ALU.add))
                    tt(A_E[:, 0:P], A_E[:, 0:P], S01[:, :], ALU.mult)
                    tt(A_E[:, 2 * P:3 * P], A_E[:, 2 * P:3 * P], S01[:, :], ALU.mult).then_inc(S("sp_ready"), 1)
                    yield q0 + 8
                    y_lo(2, 2, 16 + h, 1, PT[1][:, T:2 * T].unsqueeze(1), h + 1)

            def gmlp():
                yield S5Q + 75
                dve.wait_ge(S("s5_g_hi"), 1)
                tt(YL[:, 8:16, :], GS, YH[:, 8:16, :].bitcast(F32), ALU.subtract).then_inc(S("s5_g_split"), 1)
                yield GQ - 3
                dve.wait_ge(S("gm_squares"), 2)
                ts(rs, ss, 1.0 / 1024, EPS, ALU.mult, ALU.add).then_inc(S("gm_ms"), 1)
                yield GQ - 2
                dve.wait_ge(S("gm_root"), 1)
                chain(nc.vector.reciprocal(rs, rs))
                dve.wait_ge(S("gm_gain_in"), 16)
                for t in range(NT):
                    yield GQ - 1 + t
                    stt(GV[:, t, :], GV[:, t, :], rs[:, t:t + 1], GMG, ALU.mult, ALU.mult).then_inc(S("gm_normed"), 1)
                for n in range(4):
                    yield GQ + 2 * n + 2
                    t, g0 = n // 2, 4 * (n % 2)
                    dve.wait_ge(S("gm_mixed"), n + 1)
                    dve.wait_ge(evict["act"], find[(2, "u", 1)].evicted)
                    for g in range(4):
                        uu = GU[:, t, P * (g0 + g):P * (g0 + g) + P]
                        ins = stt(uu, PU[n % 2][:, P * g:P * g + P], gm_b[:, g0 + g:g0 + g + 1], uu, ALU.add, ALU.mult)
                    ins.then_inc(S("gm_y"), 1)
                for n in range(4):
                    yield GQ + 10 + 2 * n
                    y_lo(2, 0, 2 * n, 2, PU[n % 2].rearrange("p (k t) -> p k t", t=T), n + 1)

            def glu_out():
                for i in range(4):
                    yield n_a[2] + GLUQ[i] + 2
                    g = GS[:, 2 * i:2 * i + 2, :]
                    dve.wait_ge(S("glu_sig"), i + 1)
                    tt(g, g, SG[:, 2 * i:2 * i + 2, :], ALU.mult).then_inc(S("glu_y"), 1)
                    yield n_a[2] + GLUQ[i] + 3
                    y_lo(2, 1, 8 + 2 * i, 2, g, i + 1)

            def mlp(b):
                H0, base_evict = ts0[b] + 24, down0[b]

                def square(n):
                    dve.wait_ge(S(f"relu{b}_ready"), n + 1)
                    tt(HB[1], HB[0], HB[0], ALU.mult).then_inc(S(f"hidden{b}_ready"), 1)

                def add(base, n):
                    dve.wait_ge(used, base + (8 + 2 * n + 2))
                    for t in range(NT):
                        x = X[:, t, CH * n:CH * n + CH]
                        ins = tt(x, PA[n % 2][t], x, ALU.add)
                    ins.then_inc(evict["dve"], 1)

                def split_pair(j, r):
                    split_lo(j * 2 + (H0 + r), r, YH[:, UK * r:UK * r + UK, :], YL[:, UK * r:UK * r + UK, :])

                def body(j, first):
                    base, last = mlp_base(b, j), mlp_base(b, j - 1)
                    lo(base, 0)
                    lo(base, 1)
                    if not first:
                        add(last, 2)
                    lo(base, 2)
                    lo(base, 3)
                    if first:
                        square(0)
                    else:
                        add(last, 3)
                    for i in range(4, 7):
                        lo(base, i)
                    split_pair(j, 0)
                    split_pair(j, 1)
                    for i in range(7, 12):
                        lo(base, i)
                    square(j + 1)
                    lo(base, 12)
                    lo(base, 13)
                    add(base, 0)
                    lo(base, 14)
                    lo(base, 15)
                    add(base, 1)

                lo_upto(u0[b, "m"] + 8)
                body(0, True)
                with dve.Fori(1, NF - 1) as j:
                    body(j, False)
                base, last = mlp_base(b, NF - 1), mlp_base(b, NF - 2)
                lo(base, 0)
                lo(base, 1)
                add(last, 2)
                lo(base, 2)
                lo(base, 3)
                add(last, 3)
                split_pair(NF - 1, 0)
                split_pair(NF - 1, 1)
                lo(base, 4)
                lo(base, 5)
                add(base - 8, 0)
                lo(base, 6)
                lo(base, 7)
                add(base - 8, 1)
                add(base - 8, 2)
                st["lo"] = base + 8
                if b != blocks[-1]:
                    lo_upto(base + 8 + 3)
                add(base - 8, 3)

            for b in blocks:
                norm()
                lo_upto(u0[b, "a"] + RING)
                for i in range(8):
                    split_lo(ts0[b] + i, i % 2, XH[:, UK * i:UK * i + UK, :], XL[:, UK * i:UK * i + UK, :])
                gens = [Steps(g) for g in ([evictions(b)] + (
                    [vectors(), attn1(), lru(), pool(), sconv(), s5_params()] if b == 1 else [s5(), attn2(), gmlp(), glu_out()]) + [merge_lo(b)])]
                for p_ in range(u0[b, "m"] - u0[b, "a"]):
                    lo_upto(u0[b, "a"] + p_ + 1)
                    for g in gens:
                        g.upto(p_)
                lo_upto(u0[b, "m"] + RING - 1)
                for g in gens:
                    g.upto(10 ** 6)
                norm()
                lo_upto(u0[b, "m"] + RING)
                for i in range(8):
                    split_lo(ts0[b] + 16 + i, i % 2, XH[:, UK * i:UK * i + UK, :], XL[:, UK * i:UK * i + UK, :])
                mlp(b)
            norm()

        @block.tensor
        def _(pe):
            st = {"norm": 0, "sb": 0, "s5_out": 0}

            def mm(out_, l, r, start=True, stop=True, **kw):
                return nc.tensor.matmul(out_, l, r, start=start, stop=stop, **kw)

            def tr(out_, in_):
                return nc.tensor.transpose(out_, in_, ident[:, :])

            def unit(base, i, lh, ll, kt, acc, first, last):
                pe.wait_ge(lo_done, base + (i + 1))
                for k in range(UK):
                    for t in range(NT):
                        for n, (l, w) in enumerate(((lh, whi), (lh, wlo), (ll, whi))):
                            ins = mm(acc[t], l[:, kt + k, P * t:P * t + P], w[:, i % RING, CH * k:CH * k + CH],
                                     start=first and k == 0 and n == 0, stop=last and k == UK - 1 and n == 2)
                ins.then_inc(used, 1)

            def pair(q, r, src, c0):
                for k in range(UK):
                    for t in range(NT):
                        ins = tr(PT[r][:, T * k + P * t:T * k + P * t + P], src[:, t, c0 + P * k:c0 + P * k + P])
                ins.then_inc(ts_ready, 1)

            def norm(first):
                st["norm"] += 1
                for i in range(8):
                    if i in (4, 6):
                        yield (i - 4) // 2
                    pe.wait_ge(S("normed"), NCH * (st["norm"] - 1) + i // 2 + 1)
                    if first + i >= 2:
                        pe.wait_ge(ts_split, first + i - 1)
                    pair(first + i, i % 2, XN, 2 * P * i)

            def vectors():
                yield 3
                pe.wait_ge(S("masks_ready"), 1)
                pe.wait_ge(S("dt_rows"), 1)
                pe.wait_ge(ts_split, ts0[1] + 8)
                tr(PT[0][:, 0:P], slot(Z, 0)[:, 0:P])
                nc.tensor.transpose(PT[0][:, P:P + 96], slot(Z, 0)[0:96, P:2 * P], ident[0:96, 0:96])\
                    .then_inc(S("vectors_mm"), 1)

            def stage_transposes(b):
                stages = 0
                for n, (tag, t, q) in enumerate(TP[b]):
                    yield q
                    if b == 1 and tag in "qk":
                        src = {"q": Q1, "k": K1}[tag]
                        pe.wait_ge(S("qk_normed"), 1 if tag == "q" else 2)
                    else:
                        src = ST[stages // 2 % 2]
                        pe.wait_ge(evict["act"], find[(b, tag, 0) if b == 1 else (b,) + tag].evicted)
                        stages += 1
                    if sbase[b] + n > 0:
                        pe.wait_ge(S("stage_copied"), sbase[b] + n)
                    if b == 1:
                        if n == 0:
                            pe.wait_ge(S("cumT_ready"), 1)
                        before = sum(lq < q for lq in LRUQ)
                        if before:
                            pe.wait_ge(S("lru_exp"), before)
                    for f in range(4):
                        ins = tr(TBANK[b][:, P * f:P * f + P], src[:, t, P * f:P * f + P])
                    ins.then_inc(S("stage_transposed"), 1)

            def lru():
                yield 7
                pe.wait_ge(S("wf_split"), 1)
                for k in range(KD):
                    for n, (x, w) in enumerate(((XH, wfh), (XH, wfl), (XL, wfh))):
                        ins = mm(PU[1][0:8, 0:T], w[:, k, :], x[:, k, :], start=k == 0 and n == 0,
                                 stop=k == KD - 1 and n == 2)
                ins.then_inc(S("f_mm"), 1)
                yield 9
                pe.wait_ge(S("f_copied"), 1)
                for t in range(NT):
                    ins = nc.tensor.transpose(PU[1][:, 8 * t:8 * t + 8], CUMT[:, P * t:P * t + P], ident[0:8, 0:8])
                ins.then_inc(S("f_transposed"), 1)
                yield 13
                pe.wait_ge(S("log_f"), 1)
                pe.wait_ge(S("masks_ready"), 1)
                mm(PU[1][0:8, 0:T], LS[:, 0:8], UP[:, :])
                mm(PU[1][0:8, P:T], LS[:, 8:16], UP[:, 0:P], start=False, skip_group_check=True).then_inc(S("cum_mm"), 1)
                for f in range(4):
                    yield LRUQ[f]
                    pe.wait_ge(S("lru_u"), 1)
                    pe.wait_ge(S("small1_in"), 16 * 5)
                    pe.wait_ge(S("stage_copied"), sum(q < LRUQ[f] for _, _, q in TP[1]))
                    for w in range(2):
                        ins = mm(PU[1][:, T * w:T * w + T], BD[:, w, f, :], L_U[:, f, :])
                    ins.then_inc(S("lru_mm"), 1)
                for h in range(2):
                    yield PMQ[h]
                    pe.wait_ge(S("pool_done"), 1)
                    pe.wait_ge(S("lru_exp"), 4)
                    if h:
                        pe.wait_ge(S("pool_scaled"), 1)
                    for g in range(2):
                        ins = mm(PU[1][:, T * g:T * g + T], PW[:, 2 * h + g, :], P_X[:, 2 * h + g, :])
                    ins.then_inc(S("pool_mm"), 1)

            def attn1_scores(h):
                o, i = 64 * (h % 2), h // 2
                s = PU[0]
                if h == 0:
                    pe.wait_ge(S("stage_copied"), 4)
                    pe.wait_ge(S("sel_ready"), 1)
                else:
                    pe.wait_ge(S("p_exp"), h)
                kw = dict(start=False, stop=True, skip_group_check=True)
                mm(s[:, 0:P], QT1[o:o + 64, i, 0:P], KT1[o:o + 64, i, 0:P])
                mm(s[:, P:3 * P], QT1[o:o + 64, i, P:T], KT1[o:o + 64, i, :], **kw)
                mm(s[:, 0:P], ident[:, :], CM[:, :], **kw)
                mm(s[:, 2 * P:3 * P], ident[:, :], CM[:, :], **kw)
                mm(s[:, 0:P], SEL[:, h, :], CUMT[:, 0:P], **kw)
                mm(s[:, P:3 * P], SEL[:, h, :], CUMT[:, :], **kw)\
                    .then_inc(S("scored"), 1)

            def attn1():
                for h in range(8):
                    q0 = HQ1 + 5 * h
                    if h == 0:
                        yield q0
                        attn1_scores(0)
                    yield q0 + 4
                    pe.wait_ge(S("p_ready"), h + 1)
                    if h:
                        pe.wait_ge(S("pT_ready"), h)
                    for i in range(3):
                        ins = tr(PT[0][:, P * i:P * i + P], PB[h % 2][:, P * i:P * i + P])
                    ins.then_inc(S("p_transposed"), 1)
                    if h + 1 < 8:
                        yield q0 + 5
                        attn1_scores(h + 1)
                    yield q0 + 6
                    pe.wait_ge(S("pT_ready"), h + 1)
                    pe.wait_ge(evict["act"], find[(1, "v", 0)].evicted)
                    i, o = h // 2, 64 * (h % 2)
                    if i >= 1:
                        pe.wait_ge(yready(1, 3), i)
                    y = PT[1][o:o + 64, T * (i % 2):T * (i % 2) + T]
                    mm(y, V1[:, 0, 64 * h:64 * h + 64], PTB[h % 2][:, 0:T])
                    mm(y[:, P:T], V1[:, 1, 64 * h:64 * h + 64], PTB[h % 2][:, T:3 * P], start=False,
                       skip_group_check=True)\
                        .then_inc(S("attn_mm"), 1)

            def s5():
                for n in range(10):
                    yield BQ[n]
                    src, i = MT_SRC[n]
                    if n:
                        pe.wait_ge(S("s5_mT_copied"), n)
                    pe.wait_ge(S("c_pad"), 1)
                    if n >= 4:
                        pe.wait_ge(S("b_pad"), 1)
                    if n >= 8:
                        pe.wait_ge(S("gm_w_tril"), 1)
                    for f in range(4):
                        ins = tr(PT[1][:, P * f:P * f + P], src[:, CH * i + P * f:CH * i + P * f + P])
                    ins.then_inc(S("s5_mT"), 1)

            def s5_in():
                for j in range(32):
                    yield S5Q + 2 * j
                    i, c = j // 4, 32 * (j % 4)
                    if j == 0:
                        pe.wait_ge(S("s5_mT_copied"), 8)
                        pe.wait_ge(S("stage_copied"), sbase[2] + 4)
                    if j >= 2:
                        pe.wait_ge(S("s5_bu_read"), j - 1)
                    for r in range(2):
                        ins = mm(PU[j % 2][:, T * r:T * r + T], BT[r][c:c + 32, i, :], XI[c:c + 32, i, :],
                                 tile_position=(c, 0))
                    ins.then_inc(S("bu_mm"), 1)

            def s5_out():
                for j in range(32):
                    yield S5Q + 2 * j + 7
                    i, c = j // 4, 32 * (j % 4)
                    pe.wait_ge(S("s5_state_ready"), j + 1)
                    if j == 0:
                        pe.wait_ge(S("s5_mT_copied"), 10)
                    if j % 4 == 0 and i:
                        pe.wait_ge(S("s5_y"), i)
                    if st["sb"]:
                        pe.wait_ge(yready(2, 2), st["sb"])
                    for r in range(2):
                        ins = mm(PT[1][c:c + 32, 0:T], CT[r][:, i, c:c + 32], STATE[j % 2][:, r, :], start=r == 0, stop=r == 1,
                                 tile_position=(0, c))
                    ins.then_inc(S("s5_read"), 1)
                    st["s5_out"] = j + 1

            def attn2():
                z = PT[0]
                for h in range(8):
                    q0 = HQ2 + 6 * h
                    yield q0
                    if h == 0:
                        pe.wait_ge(S("stage_copied"), sbase[2] + 12)
                        pe.wait_ge(S("masks_ready"), 1)
                    else:
                        pe.wait_ge(S("sb_w"), h)
                    mm(z[:, 0:T], KT2[:, h, 0:P], QT2[:, h, :])
                    mm(z[:, T:3 * P], KT2[:, h, P:T], QT2[:, h, P:T], start=False, skip_group_check=True)\
                        .then_inc(S("z_mm"), 1)
                    yield q0 + 3
                    pe.wait_ge(S("sp_ready"), h + 1)
                    kw = dict(start=False, stop=True, skip_group_check=True)
                    mm(z[:, 0:T], NLOW[:, :], A_E[:, 0:T], **kw)
                    mm(z[:, P:T], NONE[:, :], A_E[:, T:3 * P], **kw)
                    mm(z[:, T:3 * P], NLOW[:, :], A_E[:, T:3 * P], **kw)
                    mm(z[:, 0:P], ident[:, :], SM[:, :], **kw)
                    mm(z[:, T:3 * P], ident[:, :], SM[:, :], **kw).then_inc(S("tri_mm"), 1)
                    yield q0 + 6
                    pe.wait_ge(S("sb_w"), h + 1)
                    pe.wait_ge(evict["act"], find[(2, "v", h // 4)].evicted)
                    if h:
                        pe.wait_ge(yready(2, 2), h)
                    if st["s5_out"] >= 4:
                        pe.wait_ge(S("s5_y"), st["s5_out"] // 4)
                    y = PT[1][:, T:2 * T]
                    mm(y, VT[:, 0, P * h:P * h + P], A_W[:, 0:T])
                    mm(y[:, P:T], VT[:, 1, P * h:P * h + P], A_W[:, T:3 * P], start=False,
                       skip_group_check=True).then_inc(S("sb_mm"), 1)
                    st["sb"] = h + 1

            def gmlp():
                for n in range(4):
                    yield GQ + 2 * n
                    t, g0 = n // 2, 4 * (n % 2)
                    pe.wait_ge(S("gm_normed"), 2)
                    if n >= 2:
                        pe.wait_ge(S("gm_y"), n - 1)
                    for g in range(4):
                        ins = mm(PU[n % 2][:, P * g:P * g + P], GW[:, g0 + g, :], GV[:, t, P * (g0 + g):P * (g0 + g) + P])
                    ins.then_inc(S("gm_mixed"), 1)
                for n in range(4):
                    yield GQ + 8 + 2 * n
                    pe.wait_ge(S("gm_y"), 4)
                    if n >= 2:
                        pe.wait_ge(yready(2, 0), n - 1)
                    for k in range(UK):
                        for t in range(NT):
                            ins = tr(PU[n % 2][:, T * k + P * t:T * k + P * t + P],
                                     GU[:, t, P * (2 * n + k):P * (2 * n + k) + P])
                    ins.then_inc(S("gm_T"), 1)

            def glu_out():
                for i in range(4):
                    yield n_a[2] + GLUQ[i]
                    pe.wait_ge(evict["act"], find[(2, "glu", i // 2)].evicted)
                    if i >= 2:
                        pe.wait_ge(S("glu_sig"), i - 1)
                    else:
                        pe.wait_ge(yready(2, 2), 8)
                    for k in range(UK):
                        for t in range(NT):
                            ins = tr(PT[i % 2][:, T * k + P * t:T * k + P * t + P],
                                     ST[i // 2][:, t, P * (2 * (i % 2) + k):P * (2 * (i % 2) + k) + P])
                    ins.then_inc(S("glu_T"), 1)

            def merge(b, before):
                for i, q in enumerate(merge_positions(b)):
                    if i == 6:
                        yield q - 4
                        pe.wait_ge(ts_split, ts0[b] + 14)
                    yield q
                    pe.wait_ge(S("tmp_added"), before + (gates_of(b) - 1) * (i // 2 + 1))
                    if i == 0 and b == 2:
                        pe.wait_ge(S("glu_sig"), 4)
                    g = ts0[b] + 8 + i
                    pe.wait_ge(ts_split, g - 1)
                    pair(g, i % 2, M, 2 * P * i)
                yield q + 2
                pe.wait_ge(ts_split, ts0[b] + 16)

            def mlp(b):
                H0, e0 = ts0[b] + 24, down0[b]
                H1, H2 = YH, YL

                def split(j, r):
                    pe.wait_ge(ts_split, j * 2 + (H0 + r - 1))
                    pair(None, r, HB[1], 2 * P * r)

                def down(j, base, i0):
                    pe.wait_ge(ts_split, j * 2 + (H0 + 2))
                    for i in range(8):
                        n = i // 2
                        if i % 2 == 0:
                            pe.wait_ge(evict["dve"], j * 4 + (e0 + n - 1))
                        unit(base, i0 + i, H1, H2, UK * (i % 2), PA[n % 2], i % 2 == 0, i % 2 == 1)

                def body(j):
                    base = mlp_base(b, j)
                    pe.wait_ge(S(f"relu{b}_ready"), j + 1)
                    for i in range(4):
                        unit(base, i, XH, XL, UK * i, PU, i == 0, False)
                    pe.wait_ge(S(f"hidden{b}_ready"), j + 1)
                    split(j, 0)
                    split(j, 1)
                    for i in range(4, 8):
                        unit(base, i, XH, XL, UK * i, PU, False, i == 7)
                    down(j, base, 8)

                pairs = Steps(norm(ts0[b] + 16))
                for i in range(8):
                    pe.wait_ge(ts_split, ts0[b] + 16 + i + 1)
                    unit(0, u0[b, "m"] + i, XH, XL, UK * i, PU, i == 0, i == 7)
                    pairs.upto(i)
                with pe.Fori(0, NF - 1) as j:
                    body(j)
                pe.wait_ge(S(f"hidden{b}_ready"), NF)
                split(NF - 1, 0)
                split(NF - 1, 1)
                down(NF - 1, mlp_base(b, NF - 1), 0)

            pe.wait_ge(S("masks_ready"), 1)
            before = 0
            for b in blocks:
                pairs = Steps(norm(ts0[b]))
                gens = [Steps(g) for g in ([stage_transposes(b)] + (
                    [vectors(), lru(), attn1()] if b == 1 else [s5(), s5_in(), s5_out(), attn2(), gmlp(), glu_out()])
                    + [merge(b, before)])]
                before += NCH * (gates_of(b) - 1)
                for ch in plan[b, "a"] + plan[b, "b"]:
                    if ch.n >= 2 and chunks[ch.n - 2] is not None:
                        pe.wait_ge(evict[chunks[ch.n - 2].by], chunks[ch.n - 2].evicted)
                    if ch.tag[0] == "prod":
                        pe.wait_ge(yready(b, ch.tag[2]), YN[b, ch.tag[2]])
                    if ch.tag[0] == "glu":
                        pe.wait_ge(S("s5_g_split"), 1)
                    lh, ll = (XH, XL) if ch.lhs == "X" else (YH, YL)
                    for i in range(ch.nu):
                        if ch.u0 == u0[b, "a"]:
                            pe.wait_ge(ts_split, ts0[b] + i + 1)
                        unit(0, ch.u0 + i, lh, ll, ch.l0 + UK * i, PA[ch.n % 2], i == 0, i == ch.nu - 1)
                        for g in [pairs] + gens:
                            g.upto(ch.u0 + i - u0[b, "a"])
                mlp(b)


_INS = ["x", "norm_mix_g", "w_in", "lru_conv_w", "lru_conv_b", "lru_wr", "lru_br", "lru_wi", "lru_bi", "lru_lambda",
        "pool_w", "pool_scale", "sconv_w", "q_norm_g", "k_norm_g", "forget_b", "w_branch", "w_out", "norm_mlp_g",
        "w_mlp_up", "w_mlp_down", "norm1_g_2", "w_in_2", "b_gate_2", "gm_norm_g_2", "gm_w_s_2", "gm_b_s_2",
        "s5_lambda_re_2", "s5_lambda_im_2", "s5_log_dt_2", "s5_b_re_2", "s5_b_im_2", "s5_c_re_2", "s5_c_im_2",
        "s5_d_2", "s5_w_glu_2", "s5_b_glu_2", "w_branch_2", "w_out_2", "norm2_g_2", "w_mlp_in_2", "w_mlp_out_2",
        "final_g_2"]


def kernel(**inputs):
    import numpy as _np
    import concourse.bacc as _bacc
    from concourse import mybir as _mybir
    from concourse.bass_utils import run_bass_kernel_spmd as _run

    nc = _bacc.Bacc("TRN2", target_bir_lowering=False, num_devices=1)
    arrays, aps = {}, {}
    for name in _INS:
        a = _np.ascontiguousarray(inputs[name])
        arrays[f"in_{name}"] = a
        aps[name] = nc.dram_tensor(f"in_{name}", a.shape, _mybir.dt.from_np(a.dtype), kind="ExternalInput").ap()
    aps["tables"] = nc.dram_tensor("tables", (32, 128, 2, T), _mybir.dt.float32, kind="Internal").ap()
    aps["x1"] = nc.dram_tensor("x1", (T, D), _mybir.dt.float32, kind="Internal").ap()
    out = nc.dram_tensor("out_0", (1, T, D), _mybir.dt.float32, kind="ExternalOutput").ap()
    build(nc, aps, out)
    r = _run(nc, [arrays], core_ids=[0])
    return r.results[0]["out_0"]
```
